# Optimizing a Trainium2 kernel written in Bass

```python
import math
import jax, jax.numpy as jnp
from jax import lax
import numpy as np

D_MODEL = 1024
BATCH = 1
SEQ = 512
DEPTH = 1

N_HEADS_A = 8
HEAD_DIM_A = 64
N_IDX_HEADS = 16
IDX_DIM = 64
TOPK_MAX = 256
N_HEADS_B = 8
QK_NOPE_DIM = 64
QK_ROPE_DIM = 32
V_DIM_B = 64
Q_LORA = 384
KV_LORA = 256
D_MIX = N_HEADS_A * HEAD_DIM_A + N_HEADS_B * V_DIM_B
D_FF = 2816
ROPE_THETA = 10000.0
EPS = 1e-6
Q_BLOCK = 128

PROJ_SIZES = (
    N_HEADS_A * HEAD_DIM_A,
    HEAD_DIM_A,
    HEAD_DIM_A,
    N_IDX_HEADS * IDX_DIM,
    IDX_DIM,
    N_IDX_HEADS,
    Q_LORA,
    KV_LORA,
    QK_ROPE_DIM,
)
D_PROJ = sum(PROJ_SIZES)


def rmsnorm(x, g):
    xf = x.astype(jnp.float32)
    y = xf * lax.rsqrt(jnp.mean(xf * xf, axis=-1, keepdims=True) + EPS)
    return (y * g.astype(jnp.float32)).astype(x.dtype)

def swiglu(x, w_gate, w_up, w_down):
    return (jax.nn.silu(x @ w_gate) * (x @ w_up)) @ w_down

def rope_tables(seq_len, dim):
    pos = jnp.arange(seq_len, dtype=jnp.float32)
    inv_freq = ROPE_THETA ** (-jnp.arange(0, dim, 2, dtype=jnp.float32) / dim)
    ang = pos[:, None] * inv_freq[None, :]
    return jnp.cos(ang), jnp.sin(ang)

def apply_rope(x, cos, sin):
    shape = (cos.shape[0],) + (1,) * (x.ndim - 3) + (cos.shape[1],)
    c = cos.reshape(shape)
    s = sin.reshape(shape)
    xf = x.astype(jnp.float32)
    x1, x2 = jnp.split(xf, 2, axis=-1)
    return jnp.concatenate([x1 * c - x2 * s, x1 * s + x2 * c], axis=-1).astype(x.dtype)

def block_slice(a, start):
    return lax.dynamic_slice_in_dim(a, start, Q_BLOCK, axis=1)

def dsa_sparse_attention(q, k, v, q_idx, k_idx, w_idx):
    B, T = q.shape[0], q.shape[1]
    top_k = min(TOPK_MAX, T // 4)
    n_blocks = T // Q_BLOCK
    key_pos = jnp.arange(T)
    scale = HEAD_DIM_A ** -0.5
    idx_scale = (N_IDX_HEADS * IDX_DIM) ** -0.5

    def one_block(i):
        s0 = i * Q_BLOCK
        qb = block_slice(q, s0)
        qib = block_slice(q_idx, s0)
        wb = block_slice(w_idx, s0).astype(jnp.float32) * idx_scale
        qpos = s0 + jnp.arange(Q_BLOCK)
        causal = key_pos[None, :] <= qpos[:, None]
        idx_logits = jnp.einsum('bqhd,bsd->bqhs', qib, k_idx).astype(jnp.float32)
        score = jnp.einsum('bqh,bqhs->bqs', wb, jax.nn.relu(idx_logits))
        score = jnp.where(causal[None], score, -jnp.inf)
        _, sel = lax.top_k(score, top_k)
        valid = sel <= qpos[None, :, None]
        kg = jax.vmap(lambda kb, ib: kb[ib])(k, sel)
        vg = jax.vmap(lambda vb, ib: vb[ib])(v, sel)
        att = jnp.einsum('bqhd,bqkd->bqhk', qb, kg).astype(jnp.float32) * scale
        att = jnp.where(valid[:, :, None, :], att, -jnp.inf)
        p = jax.nn.softmax(att, axis=-1)
        return jnp.einsum('bqhk,bqkd->bqhd', p.astype(vg.dtype), vg)

    out = lax.map(one_block, jnp.arange(n_blocks))
    return jnp.moveaxis(out, 0, 1).reshape(B, T, N_HEADS_A * HEAD_DIM_A)

def mla_attention(c_q, c_kv, k_rope, g_q_lat, g_kv_lat, w_uq, w_ukv, cos_b, sin_b):
    B, T = c_q.shape[0], c_q.shape[1]
    n_blocks = T // Q_BLOCK
    key_pos = jnp.arange(T)
    scale = (QK_NOPE_DIM + QK_ROPE_DIM) ** -0.5
    q = (rmsnorm(c_q, g_q_lat) @ w_uq).reshape(B, T, N_HEADS_B, QK_NOPE_DIM + QK_ROPE_DIM)
    q_nope, q_pe = q[..., :QK_NOPE_DIM], q[..., QK_NOPE_DIM:]
    q_pe = apply_rope(q_pe, cos_b, sin_b)
    kv = (rmsnorm(c_kv, g_kv_lat) @ w_ukv).reshape(B, T, N_HEADS_B, QK_NOPE_DIM + V_DIM_B)
    k_nope, v = kv[..., :QK_NOPE_DIM], kv[..., QK_NOPE_DIM:]
    k_pe = apply_rope(k_rope, cos_b, sin_b)

    def one_block(i):
        s0 = i * Q_BLOCK
        qn = block_slice(q_nope, s0)
        qp = block_slice(q_pe, s0)
        qpos = s0 + jnp.arange(Q_BLOCK)
        causal = key_pos[None, :] <= qpos[:, None]
        s = (jnp.einsum('bqhd,bshd->bhqs', qn, k_nope)
             + jnp.einsum('bqhr,bsr->bhqs', qp, k_pe)).astype(jnp.float32) * scale
        s = jnp.where(causal[None, None], s, -jnp.inf)
        p = jax.nn.softmax(s, axis=-1)
        return jnp.einsum('bhqs,bshd->bqhd', p.astype(v.dtype), v)

    out = lax.map(one_block, jnp.arange(n_blocks))
    return jnp.moveaxis(out, 0, 1).reshape(B, T, N_HEADS_B * V_DIM_B)

def first_inputs(seed: int = 0) -> dict:
    key = jax.random.key(seed)
    ks = jax.random.split(key, 20)

    def w(k, shape, fan_in):
        return jax.random.normal(k, shape, jnp.float32) * (fan_in ** -0.5)

    def gain(k, shape):
        return 1.0 + 0.1 * jax.random.normal(k, shape, jnp.float32)

    L = DEPTH
    return {
        "x": jax.random.normal(ks[0], (BATCH, SEQ, D_MODEL), jnp.float32),
        "g_ffn1": gain(ks[1], (L, D_MODEL)),
        "w1_gate": w(ks[2], (L, D_MODEL, D_FF), D_MODEL),
        "w1_up": w(ks[3], (L, D_MODEL, D_FF), D_MODEL),
        "w1_down": w(ks[4], (L, D_FF, D_MODEL), D_FF),
        "g_mix": gain(ks[5], (L, D_MODEL)),
        "w_in": w(ks[6], (L, D_MODEL, D_PROJ), D_MODEL),
        "g_q_lat": gain(ks[7], (L, Q_LORA)),
        "g_kv_lat": gain(ks[8], (L, KV_LORA)),
        "w_uq": w(ks[9], (L, Q_LORA, N_HEADS_B * (QK_NOPE_DIM + QK_ROPE_DIM)), Q_LORA),
        "w_ukv": w(ks[10], (L, KV_LORA, N_HEADS_B * (QK_NOPE_DIM + V_DIM_B)), KV_LORA),
        "w_out": w(ks[11], (L, D_MIX, D_MODEL), D_MIX),
        "g_ffn2": gain(ks[12], (L, D_MODEL)),
        "w2_gate": w(ks[13], (L, D_MODEL, D_FF), D_MODEL),
        "w2_up": w(ks[14], (L, D_MODEL, D_FF), D_MODEL),
        "w2_down": w(ks[15], (L, D_FF, D_MODEL), D_FF),
        "g_final": gain(ks[16], (D_MODEL,)),
    }

def first_block(x, g_ffn1, w1_gate, w1_up, w1_down, g_mix, w_in, g_q_lat, g_kv_lat,
              w_uq, w_ukv, w_out, g_ffn2, w2_gate, w2_up, w2_down, g_final):
    B, T, _ = x.shape
    cos_a, sin_a = rope_tables(T, HEAD_DIM_A)
    cos_i, sin_i = rope_tables(T, IDX_DIM)
    cos_b, sin_b = rope_tables(T, QK_ROPE_DIM)
    split_points = [int(v) for v in np.cumsum(PROJ_SIZES)[:-1]]
    for l in range(DEPTH):
        x = x + 0.5 * swiglu(rmsnorm(x, g_ffn1[l]), w1_gate[l], w1_up[l], w1_down[l])
        h = rmsnorm(x, g_mix[l])
        p = h @ w_in[l]
        qa, ka, va, qi, ki, wi, cq, ckv, kr = jnp.split(p, split_points, axis=-1)
        qa = apply_rope(qa.reshape(B, T, N_HEADS_A, HEAD_DIM_A), cos_a, sin_a)
        ka = apply_rope(ka, cos_a, sin_a)
        qi = apply_rope(qi.reshape(B, T, N_IDX_HEADS, IDX_DIM), cos_i, sin_i)
        ki = apply_rope(ki, cos_i, sin_i)
        out_a = dsa_sparse_attention(qa, ka, va, qi, ki, wi)
        out_b = mla_attention(cq, ckv, kr, g_q_lat[l], g_kv_lat[l], w_uq[l], w_ukv[l], cos_b, sin_b)
        x = x + jnp.concatenate([out_a, out_b], axis=-1) @ w_out[l]
        x = x + 0.5 * swiglu(rmsnorm(x, g_ffn2[l]), w2_gate[l], w2_up[l], w2_down[l])
    return rmsnorm(x, g_final)


CTX_LEN = 256
GRID_W = 64
D_CONV = 1024
CONV_W = 3
N_Q_HEADS = 8
N_KV_HEADS = 2
HEAD_DIM = 128
GROUP = N_Q_HEADS // N_KV_HEADS
N_MOD = 9

Q_W = N_Q_HEADS * HEAD_DIM
KV_W = N_KV_HEADS * HEAD_DIM
PIECE_WIDTHS = (D_CONV, D_CONV, D_CONV, Q_W, KV_W, KV_W, 2 * D_MODEL)
D_IN = int(sum(PIECE_WIDTHS))
SPLITS = tuple(int(s) for s in np.cumsum(PIECE_WIDTHS)[:-1])


def rms_norm(x, g):
    xf = x.astype(jnp.float32)
    y = xf * lax.rsqrt(jnp.mean(xf * xf, axis=-1, keepdims=True) + EPS)
    return (y * g.astype(jnp.float32)).astype(x.dtype)

def modulate(h, shift, scale):
    return h * (1.0 + scale) + shift

def swiglu_2(h, w_in, w_out):
    a, b = jnp.split(h @ w_in, 2, axis=-1)
    return (jax.nn.silu(a) * b) @ w_out

def axial_rope_tables(n_tokens):
    rows = n_tokens // GRID_W
    row = jnp.repeat(jnp.arange(rows), GRID_W).astype(jnp.float32)
    col = jnp.tile(jnp.arange(GRID_W), rows).astype(jnp.float32)
    n_freq = HEAD_DIM // 4
    inv = ROPE_THETA ** (-jnp.arange(n_freq, dtype=jnp.float32) / n_freq)
    ang = jnp.stack([row[:, None] * inv, col[:, None] * inv], axis=1)
    return jnp.cos(ang), jnp.sin(ang)

def apply_axial_rope(x, cos, sin):
    xs = x.reshape(x.shape[:3] + (2, 2, HEAD_DIM // 4))
    x1, x2 = xs[..., 0, :], xs[..., 1, :]
    c = cos[None, :, None].astype(x.dtype)
    s = sin[None, :, None].astype(x.dtype)
    out = jnp.stack([x1 * c - x2 * s, x2 * c + x1 * s], axis=-2)
    return out.reshape(x.shape)

def short_conv(u, w):
    L = u.shape[1]
    pad = CONV_W // 2
    up = jnp.pad(u, ((0, 0), (pad, pad), (0, 0)))
    y = up[:, 0:L] * w[0]
    for j in range(1, CONV_W):
        y = y + up[:, j:j + L] * w[j]
    return y

def conv_branch(bg, cg, vc, conv_w):
    return bg * short_conv(cg * vc, conv_w)

def gqa_attend(q, k, v):
    s = jnp.einsum('btkgd,blkd->bkgtl', q, k, preferred_element_type=jnp.float32) * (HEAD_DIM ** -0.5)
    p = jax.nn.softmax(s, axis=-1).astype(v.dtype)
    return jnp.einsum('bkgtl,blkd->btkgd', p, v)

def latent_attention(q_lat, k_all, v_all):
    B, S = q_lat.shape[:2]
    nblk = S // Q_BLOCK
    qb = q_lat.reshape(B, nblk, Q_BLOCK, N_KV_HEADS, GROUP, HEAD_DIM).swapaxes(0, 1)
    ob = lax.map(lambda qi: gqa_attend(qi, k_all, v_all), qb)
    return ob.swapaxes(0, 1).reshape(B, S, Q_W)

def split_heads(q, k, v, q_g, k_g):
    B, L = q.shape[:2]
    q = rms_norm(q.reshape(B, L, N_Q_HEADS, HEAD_DIM), q_g)
    k = rms_norm(k.reshape(B, L, N_KV_HEADS, HEAD_DIM), k_g)
    v = v.reshape(B, L, N_KV_HEADS, HEAD_DIM)
    return q, k, v

def merge_branches(y_conv, o_attn, gate_logits, w_bc, w_ba, w_out):
    g_conv, g_attn = jnp.split(jax.nn.sigmoid(gate_logits), 2, axis=-1)
    return (g_conv * (y_conv @ w_bc) + g_attn * (o_attn @ w_ba)) @ w_out

def second_inputs(seed: int = 0) -> dict:
    key = jax.random.key(seed)
    ks = jax.random.split(key, 24)

    def nrm(k, shape, scale):
        return jax.random.normal(k, shape, jnp.float32) * scale

    def gain(k, shape):
        return 1.0 + 0.1 * jax.random.normal(k, shape, jnp.float32)

    L = DEPTH
    return {
        "x": nrm(ks[0], (BATCH, SEQ, D_MODEL), 1.0),
        "c": nrm(ks[1], (BATCH, D_MODEL), 1.0),
        "ctx": nrm(ks[2], (BATCH, CTX_LEN, D_MODEL), 1.0),
        "c_ctx": nrm(ks[3], (D_MODEL,), 1.0),
        "w_mod": nrm(ks[4], (L, D_MODEL, N_MOD * D_MODEL), 0.5 * D_MODEL ** -0.5),
        "b_mod": nrm(ks[5], (L, N_MOD * D_MODEL), 0.02),
        "norm1_g": gain(ks[6], (L, D_MODEL)),
        "norm2_g": gain(ks[7], (L, D_MODEL)),
        "norm3_g": gain(ks[8], (L, D_MODEL)),
        "ffn1_w_in": nrm(ks[9], (L, D_MODEL, 2 * D_FF), D_MODEL ** -0.5),
        "ffn1_w_out": nrm(ks[10], (L, D_FF, D_MODEL), D_FF ** -0.5),
        "w_in": nrm(ks[11], (L, D_MODEL, D_IN), D_MODEL ** -0.5),
        "conv_w": nrm(ks[12], (L, CONV_W, D_CONV), CONV_W ** -0.5),
        "q_norm_g": gain(ks[13], (L, HEAD_DIM)),
        "k_norm_g": gain(ks[14], (L, HEAD_DIM)),
        "w_branch_conv": nrm(ks[15], (L, D_CONV, D_MODEL), D_CONV ** -0.5),
        "w_branch_attn": nrm(ks[16], (L, Q_W, D_MODEL), Q_W ** -0.5),
        "w_out": nrm(ks[17], (L, D_MODEL, D_MODEL), D_MODEL ** -0.5),
        "ffn2_w_in": nrm(ks[18], (L, D_MODEL, 2 * D_FF), D_MODEL ** -0.5),
        "ffn2_w_out": nrm(ks[19], (L, D_FF, D_MODEL), D_FF ** -0.5),
        "final_g": gain(ks[20], (D_MODEL,)),
    }

def second_block(x, c, ctx, c_ctx, w_mod, b_mod, norm1_g, norm2_g, norm3_g,
              ffn1_w_in, ffn1_w_out, w_in, conv_w, q_norm_g, k_norm_g,
              w_branch_conv, w_branch_attn, w_out, ffn2_w_in, ffn2_w_out, final_g):
    B, S, _ = x.shape
    cos, sin = axial_rope_tables(S)
    cx = ctx
    for layer in range(DEPTH):
        last = layer == DEPTH - 1
        mod_lat = (jax.nn.silu(c) @ w_mod[layer] + b_mod[layer])[:, None, :]
        mod_ctx = (jax.nn.silu(c_ctx) @ w_mod[layer] + b_mod[layer])[None, None, :]
        ml = jnp.split(mod_lat, N_MOD, axis=-1)
        mc = jnp.split(mod_ctx, N_MOD, axis=-1)

        x = x + 0.5 * ml[2] * swiglu_2(modulate(rms_norm(x, norm1_g[layer]), ml[0], ml[1]),
                                      ffn1_w_in[layer], ffn1_w_out[layer])
        cx = cx + 0.5 * mc[2] * swiglu_2(modulate(rms_norm(cx, norm1_g[layer]), mc[0], mc[1]),
                                        ffn1_w_in[layer], ffn1_w_out[layer])

        hx = modulate(rms_norm(x, norm2_g[layer]), ml[3], ml[4])
        hc = modulate(rms_norm(cx, norm2_g[layer]), mc[3], mc[4])
        bg_l, cg_l, vc_l, q_l, k_l, v_l, gt_l = jnp.split(hx @ w_in[layer], SPLITS, axis=-1)
        bg_c, cg_c, vc_c, q_c, k_c, v_c, gt_c = jnp.split(hc @ w_in[layer], SPLITS, axis=-1)

        y_conv_l = conv_branch(bg_l, cg_l, vc_l, conv_w[layer])

        q_l, k_l, v_l = split_heads(q_l, k_l, v_l, q_norm_g[layer], k_norm_g[layer])
        q_c, k_c, v_c = split_heads(q_c, k_c, v_c, q_norm_g[layer], k_norm_g[layer])
        q_l = apply_axial_rope(q_l, cos, sin)
        k_l = apply_axial_rope(k_l, cos, sin)
        k_all = jnp.concatenate([k_c, k_l], axis=1)
        v_all = jnp.concatenate([v_c, v_l], axis=1)
        o_l = latent_attention(q_l, k_all, v_all)

        x = x + ml[5] * merge_branches(y_conv_l, o_l, gt_l, w_branch_conv[layer],
                                       w_branch_attn[layer], w_out[layer])

        if not last:
            y_conv_c = conv_branch(bg_c, cg_c, vc_c, conv_w[layer])
            o_c = gqa_attend(q_c.reshape(B, cx.shape[1], N_KV_HEADS, GROUP, HEAD_DIM), k_c, v_c)
            o_c = o_c.reshape(B, cx.shape[1], Q_W)
            cx = cx + mc[5] * merge_branches(y_conv_c, o_c, gt_c, w_branch_conv[layer],
                                             w_branch_attn[layer], w_out[layer])
            cx = cx + 0.5 * mc[8] * swiglu_2(modulate(rms_norm(cx, norm3_g[layer]), mc[6], mc[7]),
                                            ffn2_w_in[layer], ffn2_w_out[layer])

        x = x + 0.5 * ml[8] * swiglu_2(modulate(rms_norm(x, norm3_g[layer]), ml[6], ml[7]),
                                      ffn2_w_in[layer], ffn2_w_out[layer])
    return rms_norm(x, final_g)


def setup_inputs(seed=0):
    out = dict(first_inputs(seed))
    for name, value in second_inputs(seed + 1).items():
        if name != "x":
            out[name + "_2"] = value
    return out


def reference(
    x, g_ffn1, w1_gate, w1_up, w1_down, g_mix, w_in, g_q_lat, g_kv_lat, w_uq, w_ukv, w_out,
    g_ffn2, w2_gate, w2_up, w2_down, g_final, c_2, ctx_2, c_ctx_2, w_mod_2, b_mod_2, norm1_g_2,
    norm2_g_2, norm3_g_2, ffn1_w_in_2, ffn1_w_out_2, w_in_2, conv_w_2, q_norm_g_2, k_norm_g_2,
    w_branch_conv_2, w_branch_attn_2, w_out_2, ffn2_w_in_2, ffn2_w_out_2, final_g_2,
):
    x = first_block(
        x, g_ffn1, w1_gate, w1_up, w1_down, g_mix, w_in, g_q_lat, g_kv_lat, w_uq, w_ukv, w_out,
        g_ffn2, w2_gate, w2_up, w2_down, g_final,
    )
    return second_block(
        x, c_2, ctx_2, c_ctx_2, w_mod_2, b_mod_2, norm1_g_2, norm2_g_2, norm3_g_2, ffn1_w_in_2,
        ffn1_w_out_2, w_in_2, conv_w_2, q_norm_g_2, k_norm_g_2, w_branch_conv_2,
        w_branch_attn_2, w_out_2, ffn2_w_in_2, ffn2_w_out_2, final_g_2,
    )


_drawn_inputs = setup_inputs


def setup_inputs(seed=0):
    import zlib

    import numpy as np

    out = dict(_drawn_inputs(seed))
    spreads = {}
    factors = {'g_q_lat': 5.279,
     'g_kv_lat': 3.717,
     'ctx_2': 8.0,
     'c_ctx_2': 3.475,
     'b_mod_2': 2.702,
     'norm1_g_2': 3.57,
     'norm3_g_2': 3.589,
     'q_norm_g_2': 8.0,
     'k_norm_g_2': 8.0}
    for name, (base, spread) in spreads.items():
        noise = np.random.default_rng([zlib.crc32(name.encode()), seed]).standard_normal(out[name].shape)
        drawn = base * np.exp(spread * noise) if base else spread * noise
        out[name] = __import__('jax').numpy.asarray(drawn.astype(out[name].dtype))
    for name, factor in factors.items():
        out[name] = (out[name] * factor).astype(out[name].dtype)
    return out
```

```python
import concourse.bass as bass
from concourse import mybir
from contextlib import ExitStack

P = 128
F32 = mybir.dt.float32
F32R = mybir.dt.float32r
ACT = mybir.ActivationFunctionType
ALU = mybir.AluOpType
AX = mybir.AxisListType
ds = bass.ds

T, TC, D, DFF = 512, 256, 1024, 2816
KD = D // P
CHUNKS = (8, 8, 6)
HMAX = max(CHUNKS)
SLOT = 16 * P
EPS = 1e-6
NMOD = 9
NEG = -1e30
NT = T // P
HA, HB = 8, 8
HC, KVC, TK = 8, 2, T + TC
IDX_HEADS, TOPK = 16, 128
W_IN_TILES = ([("qi", j, 640 + j * P) for j in range(8)] + [("misc", 0, None), ("kv", 0, 512)]
              + [("qa", j, j * P) for j in range(4)] + [("lat", j, 1744 + j * P) for j in range(5)])
MISC = ((1664, 64, 0), (2384, 32, 64), (1728, 16, 96))
assert sum(CHUNKS) * P == DFF

VEC = {}
_at = 0
for _name, _n in (("g_ffn1", 8), ("g_mix", 8), ("g_ffn2", 8), ("g_final", 8), ("g_q_lat", 3), ("g_kv_lat", 2),
                  ("norm1", 8), ("norm2", 8), ("norm3", 8), ("final", 8), ("q_norm", 1), ("k_norm", 1),
                  ("b_mod", NMOD * KD), ("conv", 24), ("c", 8), ("c_ctx", 8)):
    VEC[_name] = (_at, _n)
    _at += _n
NVEC = _at


class Count:

    def __init__(self, sem):
        self.sem, self.n, self.turn = sem, 0, 0

    def inc(self, ins):
        self.n += 1
        return ins.then_inc(self.sem, 1)

    def settle(self, eng, ins):
        self.inc(ins)
        eng.wait_ge(self.sem, self.turn + self.n)


def build(nc, inp, out):
    ctx = ExitStack()
    with ctx:
        def sb(name, shape, dt=F32, st=ctx):
            return st.enter_context(nc.sbuf_tensor(name, shape, dt))

        def sem(name):
            return ctx.enter_context(nc.semaphore(name))

        X = sb("X", [P, KD, T])
        NH = sb("NH", [P, KD, T + TC], F32R)
        NL = sb("NL", [P, KD, T + TC], F32R)
        RAW = [sb(f"RAW{s}", [P, SLOT]) for s in range(2)]
        WH = [sb(f"WH{s}", [P, SLOT], F32R) for s in range(2)]
        WL = [sb(f"WL{s}", [P, SLOT], F32R) for s in range(2)]
        ident, ones = sb("ident", [P, P]), sb("ones", [P, P])
        vecs = sb("vecs", [P, NVEC])
        eps = sb("eps", [P, 1])
        SA = sb("SA", [P, 2, T + TC])
        VA = sb("VA", [P, 2, T + TC])
        RB = sb("RB", [P, T])
        CV2 = sb("CV2", [P, KD, 2])
        MOD = sb("MOD", [P, NMOD * KD, 2])
        NM, DEN = sb("NM", [P, 4]), sb("DEN", [P, 4])
        GS = sb("GS", [P, 5, KD])
        HG = sb("HG", [P, 3, KD])
        ff = ExitStack()
        HH = sb("HH", [P, HMAX, T + TC], F32R, ff)
        HL = sb("HL", [P, HMAX, T + TC], F32R, ff)
        CX = sb("CX", [P, KD, TC], F32, ff)
        MW = [sb(f"MW{s}", [P, KD, P], F32, ff) for s in range(2)]
        ff.close()
        ld = ExitStack()
        XIN = sb("XIN", [P, T // P, D], F32, ld)
        ld.close()

        a1 = ExitStack()
        QA = sb("QA", [P, 4, T], F32, a1)
        KA = sb("KA", [P, T], F32, a1)
        KPE = sb("KPE", [P, T], F32, a1)
        VAP = sb("VAP", [P, NT, 2, P], F32, a1)
        BIAS = sb("BIAS", [P, NT - 1, T], F32, a1)
        CM = sb("CM", [P, T], F32, a1)
        TB = sb("TB", [P, 2, T], F32, a1)
        PERM = sb("PERM", [P, 4, P], F32, a1)
        M8 = sb("M8", [P, 8], F32, a1)
        early = ExitStack()
        QI = sb("QI", [P, 8, T], F32, early)
        KI = sb("KI", [P, T], F32, early)
        CQ = sb("CQ", [P, 5, T], F32, early)
        TA = sb("TA", [P, 2, T], F32, early)
        WI = sb("WI", [P, NT, IDX_HEADS], F32, early)
        early.close()
        VB = sb("VB", [P, NT, HB, P], F32, a1)
        QB, KB = sb("QB", [P, 4, T], F32, a1), sb("KB", [P, 4, T], F32, a1)
        PT = sb("PT", [P, NT * 8 * P], F32, a1)
        a1.close()

        a2 = ExitStack()
        M = sb("M", [P, KD, T], F32, a2)
        GA = sb("GA", [P, KD, T], F32, a2)
        conv = ExitStack()
        YH, YL = sb("YH", [P, KD, T], F32R, conv), sb("YL", [P, KD, T], F32R, conv)
        conv.close()
        mix = ExitStack()
        MH, ML = sb("MH", [P, KD, T], F32R, mix), sb("ML", [P, KD, T], F32R, mix)
        mix.close()
        QT = sb("QT", [P, HC, T], F32, a2)
        KT = sb("KT", [P, KVC, TK], F32, a2)
        V2 = sb("V2", [P, TK // P, KVC * P], F32, a2)
        PT2 = sb("PT2", [P, TK // P, 4, P], F32, a2)
        TX = sb("TX", [P, 2, T], F32, a2)
        PX = sb("PX", [P, P], F32, a2)
        a2.close()

        PS = ctx.enter_context(nc.psum_tensor("PS", [P, 8 * 512], F32))
        B = [PS[:, i * 512:(i + 1) * 512] for i in range(8)]
        G, U, CG, CU = (B[0], B[2]), (B[1], B[3]), (B[4], B[6]), (B[5], B[7])

        w_loaded = [sem(f"w_loaded{s}") for s in range(2)]
        w_hi, w_lo = sem("w_hi"), sem("w_lo")
        pe_done = sem("pe_done")
        psum_free = sem("psum_free")
        h_split = sem("h_split")
        gate_done = sem("gate_done")
        norm_sq, norm_mm, norm_rms = sem("norm_sq"), sem("norm_mm"), sem("norm_rms")
        norm_x, norm_hi, norm_lo = sem("norm_x"), sem("norm_hi"), sem("norm_lo")
        mod_loaded = [sem(f"mod_loaded{s}") for s in range(2)]
        mod_s = sem("mod_s")
        mod_done, mod_out = sem("mod_done"), sem("mod_out")
        x_loaded, c_loaded = sem("x_loaded"), sem("c_loaded")
        tp_done, tp_out = sem("tp_done"), sem("tp_out")
        rope_y, rope_mm, rope_out = sem("rope_y"), sem("rope_mm"), sem("rope_out")
        lat_out = sem("lat_out")
        a_loaded = sem("a_loaded")
        ix_mm, ix_relu, ix_acc = sem("ix_mm"), sem("ix_relu"), sem("ix_acc")
        v_zero, v_mm, v_out = sem("v_zero"), sem("v_mm"), sem("v_out")
        pj_mm, pj_y, pj_sw, pj_out = sem("pj_mm"), sem("pj_y"), sem("pj_sw"), sem("pj_out")
        at_s, at_m, at_e, at_r, at_t, at_c = (sem(f"at_{c}") for c in "smertc")
        at_v, at_h, at_o = sem("at_v"), sem("at_h"), sem("at_o")
        conv_s = sem("conv_s")
        y_split, y_part = sem("y_split"), sem("y_part")
        ga_done = sem("ga_done")
        hn_sq, hn_mm, hn_rms, hn_z, hn_sw, hn_out = (sem(f"hn_{c}") for c in ("sq", "mm", "rms", "z", "sw", "out"))
        b_loaded = sem("b_loaded")
        v2_mm, v2_out = sem("v2_mm"), sem("v2_out")
        at2_s, at2_m, at2_e, at2_r, at2_t, at2_c = (sem(f"at2_{c}") for c in "smertc")
        at2_v, at2_h, at2_o = sem("at2_v"), sem("at2_h"), sem("at2_o")
        mix_s = sem("mix_s")
        ctx_loaded, ctx_tp, ctx_out = sem("ctx_loaded"), sem("ctx_tp"), sem("ctx_out")
        act_s, dve_s, pool_s, c2_s = sem("act_s"), sem("dve_s"), sem("pool_s"), sem("c2_s")
        out_s = sem("out_s")

        def vec(name, k=0):
            return vecs[:, VEC[name][0] + k:VEC[name][0] + k + 1]

        dmas = []

        def plan(n, d=2):
            dmas.extend([d] * n)
            return len(dmas) - n

        def plan_ffn():
            return [(plan(c), plan(KD // 2)) for c in CHUNKS]

        def loaded(b0, u, i=0):
            return i * 32 + 16 * sum(dmas[(b0 + u) % 2:b0 + u + 1:2])

        ffn1 = plan_ffn()
        w_in_b = [plan(1, 4 if j == 4 else 1 if j == 9 else 2) for j in range(10)][0]
        v_b, pj_b = plan(1), plan(2, 3)
        wo_b = plan(KD // 2)
        ffn2 = plan_ffn()
        ffn3 = plan_ffn()
        conv_b, bg_b, gc_b, ga_b = plan(KD), plan(KD // 2), plan(KD), plan(KD // 2)
        q_b, k_b, v2_b = plan(HC // 2), plan(1), plan(1)
        ba_b, wo2_b = plan(KD // 2), plan(KD // 2)
        ffn4 = plan_ffn()
        NB = len(dmas)
        NF = DFF // P
        G0 = {"ffn1": 0, "ffn2": NF, "ffn3": 2 * NF, "conv": 3 * NF, "gc": 3 * NF + KD, "ffn4": 3 * NF + 2 * KD}
        H0 = {"ffn1": 0, "ffn2": NF, "ffn3": 2 * NF, "ffn4": 3 * NF}
        M0 = {"ffn1": 0, "wo": NF + 12, "ffn2": NF + 12 + KD // 2}
        assert M0["ffn2"] + NF + 12 == NMOD * KD
        NCTX = 5 * KD
        MACC = RB[:, :].rearrange("p (t v c) -> p t v c", t=2, v=2)

        def vectors(m0):
            return 2 if m0 < NCTX else 1

        def mod(i, k, v):
            return MOD[:, ds(k + i * KD, 1), v:v + 1].rearrange("p a b -> p (a b)")

        MODULATED = (("norm1", 1, 0), ("norm1", 1, 1), ("norm2", 4, 0), ("norm2", 4, 1), ("norm3", 7, 0))
        HALVED = ((2, 0), (2, 1), (8, 0))
        block = ctx.enter_context(nc.Block())

        def stage(eng, b0, n, straight=False):
            lead = n if straight else 2 if b0 == 0 else 0
            for j in range(lead):
                yield b0 + j, j, (b0 + j) % 2, (loaded(b0, j + 1) if b0 + j + 1 < len(dmas) else None)
            if lead < n:
                with eng.Fori(0, (n - lead) // 2) as i:
                    for u in range(lead, lead + 2):
                        yield i * 2 + (b0 + u), i * 2 + u, (b0 + u) % 2, i * 32 + loaded(b0, u + 1)

        def after(b, n):
            return None if isinstance(b, int) and b + n < 1 else b + n

        def wait(eng, s, value):
            if value is not None:
                eng.wait_ge(s, value)

        norms = []

        class Norm:
            def __init__(self, src, n, tok, gain, dst=None, shift=None, ready=None):
                self.src, self.n, self.tok, self.gain, self.dst, self.shift = src, n, tok, gain, dst, shift
                self.ready = ready
                self.base, self.no = sum(m.n for m in norms), len(norms)
                self.low = sum(m.n for m in norms if m.dst)
                norms.append(self)

        def x_src(k):
            return X[:, k, :]

        def n_dst(k):
            return NH[:, k, 0:T], NL[:, k, 0:T]

        def items_of(n):
            found = []
            for half, t in enumerate(W_IN_TILES[2 * n:2 * n + 2]):
                name, j = t[0], t[1]
                found += {"qi": [("rope", half, QI[:, j, :])] if name == "qi" else None,
                          "qa": [("rope", half, QA[:, j, :])] if name == "qa" else None,
                          "misc": [("twice", half, KI[:, :]), ("kr", half, None), ("wi", half, None)],
                          "kv": [("twice", half, KA[:, :]), ("va", half, None)], "lat": []}[name]
            return found

        ITEMS = [items_of(n) for n in range(10)]
        ITEM0 = [sum(len(x) for x in ITEMS[:n]) for n in range(11)]
        COPIED = [[h for h, t in enumerate(W_IN_TILES[2 * n:2 * n + 2]) if t[0] != "lat"] for n in range(10)]
        COPY0 = [sum(len(x) for x in COPIED[:n]) for n in range(11)]

        UNITS = [("b", h, q) for h in range(HB) for q in range(NT)] + [("a", h, q) for q in range(NT) for h in range(HA)]
        PER_GROUP = 8
        NG = len(UNITS) // PER_GROUP

        def q_scores(u):
            kind, h, q = UNITS[u]
            keys = (q + 1) * P
            if kind == "b":
                return QB[0:96, h % 4, q * P:(q + 1) * P], KB[0:96, h % 4, 0:keys], keys
            r = slice((h % 2) * 64, (h % 2) * 64 + 64)
            return QA[r, h // 2, q * P:(q + 1) * P], KA[r, 0:keys], keys

        def pt_of(u):
            kind, h, q = UNITS[u]
            if kind == "b":
                return PT[:, :].rearrange("p (h s q) -> p h s q", h=2, s=NT)[:, h % 2, 0:q + 1, q * P:(q + 1) * P]
            return PT[:, :].rearrange("p (s h q) -> p s h q", s=NT, h=8)[:, 0:q + 1, (h % 2) * 4 + h // 2, :]

        def heads_out(g, n):
            if g < 4:
                return n[:, 4 + g, 0:T]
            return n[:, 0:4, (g - 4) * P:(g - 3) * P]

        AHEAD = 3
        VF, SF = VA[:, :, :].rearrange("p a t -> p (a t)"), SA[:, :, :].rearrange("p a t -> p (a t)")

        def p_slot(u):
            return (VF[:, (u % 4) * T:(u % 4 + 1) * T] if u % 4 < 3 else SF[:, 2 * T:3 * T])

        def p_slot2(u):
            return (VA, SA)[u % 4 // 2][:, u % 2, :]

        def stat(t, u):
            return t[:, u % 4:u % 4 + 1]

        norm1 = Norm(x_src, KD, T, lambda k: vec("g_ffn1", k), n_dst, ready=lambda k: (tp_out, 25 + k))

        def stream_ready(stages):
            return lambda k: (psum_free, stages[-1][1] + k // 2 + 1)

        norm_mix = Norm(x_src, KD, T, lambda k: vec("g_mix", k), n_dst, ready=stream_ready(ffn1))
        norm_q = Norm(lambda k: CQ[:, k, :], 3, T, lambda k: vec("g_q_lat", k), n_dst,
                      ready=lambda k: (lat_out, k + 1))
        norm_kv = Norm(lambda k: CQ[:, 3 + k, :], 2, T, lambda k: vec("g_kv_lat", k), lambda k: n_dst((3, 7)[k]),
                       ready=lambda k: (lat_out, k + 4))
        norm2 = Norm(x_src, KD, T, lambda k: vec("g_ffn2", k), n_dst,
                     ready=lambda k: (psum_free, wo_b + k // 2 + 1))
        norm_final = Norm(x_src, KD, T, lambda k: vec("g_final", k), None, ready=stream_ready(ffn2))

        def c_src(k):
            return CX[:, k, :]

        def c_dst(k):
            return NH[:, k, T:T + TC], NL[:, k, T:T + TC]

        def modulated(which, src, tok, dst, ready):
            i, v = MODULATED[which][1] - 1, MODULATED[which][2]
            return Norm(src, KD, tok, lambda k: GS[:, which, k:k + 1], dst,
                        shift=lambda k: MOD[:, i * KD + k, v:v + 1], ready=ready)

        norm_x1 = modulated(0, x_src, T, n_dst, lambda k: (norm_x, norm_final.base + k + 1))
        norm_c1 = modulated(1, c_src, TC, c_dst, lambda k: (ctx_out, 2 * KD))
        norm_x2 = modulated(2, x_src, T, n_dst, stream_ready(ffn3))
        norm_c2 = modulated(3, c_src, TC, c_dst, stream_ready(ffn3))
        norm_x3 = modulated(4, x_src, T, n_dst, lambda k: (psum_free, wo2_b + k // 2 + 1))
        norm_out = Norm(x_src, KD, T, lambda k: vec("final", k), None, ready=stream_ready(ffn4))

        HN = [(q_b + j // 2, 0, j % 2, T, "q_norm", QT[:, j, :]) for j in range(HC)]
        HN += [(k_b, 0, j, T, "k_norm", KT[:, j, TC:TK]) for j in range(KVC)]
        HN += [(k_b, 1, j, TC, "k_norm", KT[:, j, 0:TC]) for j in range(KVC)]

        def hn_of(b):
            return [i for i, h in enumerate(HN) if h[0] == b]

        def hn_waves(b):
            return [hn_of(b)[w:w + 2] for w in range(0, len(hn_of(b)), 2)]

        def hn_bank(i):
            b, other, half, tok = HN[i][:4]
            return (G, U)[half][(b + other) % 2][:, 0:tok]

        UNITS2 = [(g, q, e) for g in range(KVC) for q in range(NT) for e in range(4)]

        @block.sync
        def _(sp):
            sp.dma_start(XIN[:, :, :], inp["x"][0].rearrange("(t p) d -> p t d", p=P)).then_inc(x_loaded, 16)
            for dst, src in ((ident, "ident"), (vecs, "vecs")):
                sp.dma_start(dst[:, :], inp[src]).then_inc(c_loaded, 16)

            def weights(w, k0, kn, c0, n):
                return w[k0 * P:(k0 + kn) * P, :].rearrange("(k p) n -> p k n", p=P)[:, :, ds(c0, n)]

            def mods(b0, j, s, m0):
                if m0 is None:
                    return
                t = (s + b0) % 2
                if m0 == M0["wo"]:
                    sp.wait_ge(at_o, NG)
                if not (isinstance(j, int) and j + m0 < 2):
                    sp.wait_ge(mod_s, j * KD + KD * (m0 - 1))
                sp.dma_start(MW[t][:, :, :], weights(inp["w_mod_2"][0], 0, KD, j * P + m0 * P, P))\
                    .then_inc(mod_loaded[t], 16)

            def gate_up(b0, n, wg, cg, wu, cu, m0=None):
                for b, j, s, _ in stage(sp, b0, n):
                    wait(sp, w_lo, after(b, -1))
                    raw = RAW[s][:, :].rearrange("p (h k c) -> p h k c", h=2, k=KD)
                    sp.dma_start(raw[:, 0], weights(wg, 0, KD, j * P + cg, P)).then_inc(w_loaded[s], 16)
                    sp.dma_start(raw[:, 1], weights(wu, 0, KD, j * P + cu, P)).then_inc(w_loaded[s], 16)
                    mods(b0, j, s, m0)

            def pairs(b0, n, w, k0, kn, c0, straight=False, m0=None):
                for b, j, s, _ in stage(sp, b0, n, straight):
                    wait(sp, w_lo, after(b, -1))
                    raw = RAW[s][:, 0:kn * 2 * P].rearrange("p (k c) -> p k c", k=kn)
                    h = kn // 2
                    sp.dma_start(raw[:, 0:h], weights(w, k0, h, j * (2 * P) + c0, 2 * P)).then_inc(w_loaded[s], 16)
                    sp.dma_start(raw[:, h:kn], weights(w, k0 + h, kn - h, j * (2 * P) + c0, 2 * P))\
                        .then_inc(w_loaded[s], 16)
                    mods(b0, j, s, m0)

            def ffn(stages, wg, cg, wu, cu, wd, last=False, m0=None):
                k0 = 0
                for c, (kn, (bg, bd)) in enumerate(zip(CHUNKS, stages)):
                    gate_up(bg, kn, wg, cg + k0 * P, wu, cu + k0 * P, m0)
                    m1 = None if m0 is None else m0 + kn
                    pairs(bd, KD // 2, wd, k0, kn, 0, last and c == 2, m1)
                    m0 = None if m0 is None else m1 + KD // 2
                    k0 += kn

            ffn(ffn1, inp["w1_gate"][0], 0, inp["w1_up"][0], 0, inp["w1_down"][0], m0=M0["ffn1"])
            w_in, w_uq, w_ukv = inp["w_in"][0], inp["w_uq"][0], inp["w_ukv"][0]
            for n in range(10):
                b = w_in_b + n
                s = b % 2
                sp.wait_ge(w_lo, b - 1)
                raw = RAW[s][:, :].rearrange("p (h k c) -> p h k c", h=2, k=KD)
                for half, (name, j, c) in enumerate(W_IN_TILES[2 * n:2 * n + 2]):
                    for c0, width, at in (MISC if name == "misc" else ((c, P, 0),)):
                        sp.dma_start(raw[:, half, :, at:at + width],
                                     w_in[:, c0:c0 + width].rearrange("(k p) n -> p k n", p=P)).then_inc(w_loaded[s], 16)
                if n == 0:
                    sp.wait_ge(pe_done, w_in_b)
                    sp.wait_ge(mod_s, KD * M0["wo"])
                    for dst, src in ((TA, "rope64"), (TB, "rope96"), (PERM, "perms")):
                        sp.dma_start(dst[:, :, :], inp[src]).then_inc(a_loaded, 16)
                    sp.dma_start(CM[:, :], inp["causal"]).then_inc(a_loaded, 16)
            s = v_b % 2
            sp.wait_ge(w_lo, v_b - 1)
            for k in range(2):
                sp.dma_start(RAW[s][:, k * 512:(k + 1) * 512].rearrange("p (h c) -> p h c", h=HB),
                             w_ukv[k * P:(k + 1) * P].rearrange("p (h c) -> p h c", h=HB)[:, :, 64:128])\
                    .then_inc(w_loaded[s], 16)
            for n in range(2):
                b = pj_b + n
                s = b % 2
                sp.wait_ge(w_lo, b - 1)
                sp.dma_start(RAW[s][:, 0:1152].rearrange("p (k c) -> p k c", k=3),
                             w_uq[:, n * 384:(n + 1) * 384].rearrange("(k p) n -> p k n", p=P)).then_inc(w_loaded[s], 16)
                for k in range(2):
                    sp.dma_start(RAW[s][:, 1152 + k * 256:1408 + k * 256].rearrange("p (h c) -> p h c", h=4),
                                 w_ukv[k * P:(k + 1) * P].rearrange("p (h c) -> p h c", h=HB)[:, 4 * n:4 * n + 4, 0:64])\
                        .then_inc(w_loaded[s], 16)
            pairs(wo_b, KD // 2, inp["w_out"][0], 0, KD, 0, m0=M0["wo"])
            ffn(ffn2, inp["w2_gate"][0], 0, inp["w2_up"][0], 0, inp["w2_down"][0], m0=M0["ffn2"])
            w1, w2, w_in2 = inp["ffn1_w_in_2"][0], inp["ffn2_w_in_2"][0], inp["w_in_2"][0]
            sp.wait_ge(pe_done, ffn3[0][0])
            sp.wait_ge(mod_s, KD * NMOD * KD)
            sp.dma_start(XIN[:, 0:2, :], inp["ctx_2"][0].rearrange("(t p) d -> p t d", p=P)).then_inc(ctx_loaded, 16)
            ffn(ffn3, w1, 0, w1, DFF, inp["ffn1_w_out_2"][0])
            gate_up(conv_b, KD, w_in2, D, w_in2, 2 * D)
            pairs(bg_b, KD // 2, w_in2, 0, KD, 0)
            gate_up(gc_b, KD, w_in2, 4608, inp["w_branch_conv_2"][0], 0)
            pairs(ga_b, KD // 2, w_in2, 0, KD, 4608 + D)
            sp.wait_ge(pe_done, ga_b)
            sp.dma_start(TX[:, :, :], inp["rope128"]).then_inc(b_loaded, 16)
            sp.dma_start(PX[:, :], inp["perms"][:, 0, :]).then_inc(b_loaded, 16)
            pairs(q_b, HC // 2, w_in2, 0, KD, 3072)
            pairs(k_b, 1, w_in2, 0, KD, 4096, True)
            pairs(v2_b, 1, w_in2, 0, KD, 4352, True)
            pairs(ba_b, KD // 2, inp["w_branch_attn_2"][0], 0, KD, 0)
            pairs(wo2_b, KD // 2, inp["w_out_2"][0], 0, KD, 0)
            ffn(ffn4, w2, 0, w2, DFF, inp["ffn2_w_out_2"][0], True)
            sp.wait_ge(tp_out, 32 * 2)
            sp.dma_start(out[0].rearrange("(t p) d -> p t d", p=P), XIN[:, :, :]).then_inc(out_s, 16)
            sp.wait_ge(out_s, 16)

        @block.tensor
        def _(pe):
            def transposes(src_of, no, first_waits):
                for t in range(32):
                    if t >= 4:
                        pe.wait_ge(tp_out, no * 32 + t - 3)
                    pe.transpose(B[t % 4][:, 0:P], src_of(t), ident[:, :]).then_inc(tp_done, 1)

            def norm(m, banks_free):
                for k in range(m.n):
                    if k == 0:
                        wait(pe, psum_free, banks_free)
                    pe.wait_ge(norm_sq, m.base + k + 1)
                    pe.matmul(B[7][:, 0:m.tok], ones[:, :], SA[:, k % 2, 0:m.tok],
                              start=k == 0, stop=k == m.n - 1).then_inc(norm_mm, 1)

            def begin(b):
                pe.wait_ge(w_lo, b + 1)
                wait(pe, psum_free, after(b, -1))

            def tile(outs, wt, xs, kn, ready=None):
                for k in range(kn):
                    if ready is not None:
                        pe.wait_ge(ready[0], ready[1] + k + 1)
                    wh, wl = wt(k)
                    for o, (xh, xl) in zip(outs, xs):
                        pe.matmul(o, wh, xh(k), start=k == 0, stop=False)
                        pe.matmul(o, wh, xl(k), start=False, stop=False)
                    for o, (xh, xl) in zip(outs, xs):
                        last = pe.matmul(o, wl, xh(k), start=False, stop=k == kn - 1)
                return last

            def part(h, l, a, b):
                return (lambda k: h[:, k, a:b]), (lambda k: l[:, k, a:b])

            def mods(b0, j, s, m0):
                if m0 is None:
                    return
                t = (s + b0) % 2
                pe.wait_ge(mod_s, j * KD + KD * (m0 + 1))
                wait(pe, mod_out, after(j + m0, -1))
                for v in range(vectors(m0)):
                    last = pe.matmul(B[4 + t][:, v:v + 1], MACC[:, t, v, :], ones[:, 0:1], start=True, stop=True)
                last.then_inc(mod_done, 1)

            def gate_up(b0, n, xs, banks, ready, m0=None, xu=None, ready_u=None):
                for b, j, s, _ in stage(pe, b0, n):
                    begin(b)
                    for half in range(2):
                        def wt(k):
                            c = (half * KD + k) * P
                            return WH[s][:, c:c + P], WL[s][:, c:c + P]
                        if half and xu:
                            last = tile(banks[half][s], wt, xu, KD, ready_u)
                        else:
                            last = tile(banks[half][s], wt, xs, KD, ready)
                    last.then_inc(pe_done, 1)
                    mods(b0, j, s, m0)

            def pairs(b0, n, xs, banks, kn, ready=None, straight=False, m0=None):
                for b, j, s, _ in stage(pe, b0, n, straight):
                    begin(b)
                    for half in range(2):
                        def wt(k):
                            c = (k * 2 + half) * P
                            return WH[s][:, c:c + P], WL[s][:, c:c + P]
                        last = tile(banks[half][s], wt, xs, kn, ready)
                    last.then_inc(pe_done, 1)
                    mods(b0, j, s, m0)

            xb = [[[G[s][:, :]] for s in range(2)], [[U[s][:, :]] for s in range(2)]]
            xcb = [[[G[s][:, :], CG[s][:, 0:TC]] for s in range(2)], [[U[s][:, :], CU[s][:, 0:TC]] for s in range(2)]]
            XS = [part(NH, NL, 0, T)]
            XCS = XS + [part(NH, NL, T, T + TC)]
            HS = [part(HH, HL, 0, T)]
            HCS = HS + [part(HH, HL, T, T + TC)]

            def ffn(stages, m, h0, xs, hs, banks, last=False, m0=None):
                for c, (kn, (bg, bd)) in enumerate(zip(CHUNKS, stages)):
                    gate_up(bg, kn, xs, banks, (norm_lo, m.low) if c == 0 else None, m0)
                    m1 = None if m0 is None else m0 + kn
                    pairs(bd, KD // 2, hs, banks, kn, (h_split, h0), last and c == 2, m1)
                    m0 = None if m0 is None else m1 + KD // 2
                    h0 += kn

            pe.wait_ge(c_loaded, 32)
            pe.wait_ge(x_loaded, 16)
            pe.wait_ge(c2_s, 2)
            transposes(lambda t: XIN[:, t // KD, (t % KD) * P:(t % KD + 1) * P], 0, None)
            norm(norm1, None)
            ffn(ffn1, norm1, H0["ffn1"], XS, HS, xb, m0=M0["ffn1"])
            norm(norm_mix, w_in_b)

            def items(n):
                for i, (kind, half, _) in enumerate(ITEMS[n], ITEM0[n]):
                    y = COPY0[n] + COPIED[n].index(half)
                    src = SA[:, y % 2, 0:T]
                    pe.wait_ge(rope_y, y + 1)
                    if i >= 2:
                        pe.wait_ge(rope_out, i - 1)
                    o = B[4 + i % 2]
                    if kind in ("wi", "va"):
                        for t in range(NT):
                            last = pe.transpose(o[:, t * P:(t + 1) * P], src[:, t * P:(t + 1) * P], ident[:, :])
                    else:
                        if kind == "twice":
                            pe.matmul(B[6 + i % 2][:, :], PERM[:, 1, :], src, start=True, stop=True)
                        p = {"rope": 0, "twice": 2, "kr": 3}[kind]
                        last = pe.matmul(o[:, :], PERM[:, p, :], src, start=True, stop=True)
                    last.then_inc(rope_mm, 1)

            for n in range(10):
                b = w_in_b + n
                s = b % 2
                begin(b)
                for half in range(len(W_IN_TILES[2 * n:2 * n + 2])):
                    def wt(k):
                        c = (half * KD + k) * P
                        return WH[s][:, c:c + P], WL[s][:, c:c + P]
                    last = tile(((G, U)[half][s][:, :],), wt, XS, KD, (norm_lo, norm_mix.low))
                    if n and half == 0:
                        if n == 1:
                            pe.wait_ge(a_loaded, 64)
                        if len(W_IN_TILES[2 * n:2 * n + 2]) == 2:
                            items(n - 1)
                last.then_inc(pe_done, 1)
            pe.wait_ge(rope_out, ITEM0[10])
            norm(norm_q, v_b)
            norm(norm_kv, None)

            n = 0
            for q in range(1, NT):
                for h in range(IDX_HEADS):
                    if n >= 2:
                        pe.wait_ge(ix_relu, n - 1)
                    r = slice((h % 2) * 64, (h % 2) * 64 + 64)
                    pe.matmul(B[n % 2][:, 0:(q + 1) * P], QI[r, h // 2, q * P:(q + 1) * P], KI[r, 0:(q + 1) * P],
                              start=True, stop=True).then_inc(ix_mm, 1)
                    n += 1

            begin(v_b)
            s = v_b % 2
            for t in range(NT):
                if t >= 2:
                    pe.wait_ge(v_out, t - 1)
                if t == 0:
                    pe.wait_ge(norm_lo, norm_kv.low + 2)
                for k in range(2):
                    xh, xl = (z[:, (3, 7)[k], t * P:(t + 1) * P] for z in (NH, NL))
                    wh, wl = (z[s][:, k * 512:(k + 1) * 512] for z in (WH, WL))
                    pe.matmul(B[2 + t % 2][:, :], xh, wh, start=k == 0, stop=False)
                    pe.matmul(B[2 + t % 2][:, :], xh, wl, start=False, stop=False)
                    last = pe.matmul(B[2 + t % 2][:, :], xl, wh, start=False, stop=k == 1)
                last.then_inc(v_mm, 1)
            pe.wait_ge(v_out, NT)
            pe.sem_inc(pe_done, 1)

            def project(n):
                b = pj_b + n
                s = b % 2
                begin(b)
                for i in range(4):
                    if i or n:
                        pe.wait_ge(pj_out, 4 * n + i)
                    for k in range(3):
                        xh, xl = (z[:, k, 0:T] for z in (NH, NL))
                        wh, wl = (z[s][:, k * 384 + i * 96:k * 384 + i * 96 + 96] for z in (WH, WL))
                        pe.matmul(B[6][0:96, :], wh, xh, start=k == 0, stop=False)
                        pe.matmul(B[6][0:96, :], wh, xl, start=False, stop=False)
                        pe.matmul(B[6][0:96, :], wl, xh, start=False, stop=k == 2)
                    for k in range(2):
                        xh, xl = (z[:, (3, 7)[k], 0:T] for z in (NH, NL))
                        c = 1152 + k * 256 + i * 64
                        wh, wl = (z[s][:, c:c + 64] for z in (WH, WL))
                        pe.matmul(B[7][0:64, :], wh, xh, start=k == 0, stop=False)
                        pe.matmul(B[7][0:64, :], wh, xl, start=False, stop=False)
                        last = pe.matmul(B[7][0:64, :], wl, xh, start=False, stop=k == 1)
                    last.then_inc(pj_mm, 1)
                    pe.wait_ge(pj_y, 4 * n + i + 1)
                    if n and i == 0:
                        pe.wait_ge(at_o, 1)
                    last = pe.matmul(B[4][0:96, :], PERM[0:96, 3, 0:96], SF[0:96, (i % 2) * T:(i % 2 + 1) * T], start=True, stop=True)
                    last.then_inc(pj_sw, 1)
                pe.wait_ge(pj_sw, 4 * n + 4)
                pe.sem_inc(pe_done, 1)

            def scores(u):
                if u >= 2:
                    pe.wait_ge(at_m, u - 1)
                q, k, keys = q_scores(u)
                pe.matmul(B[u % 2][:, 0:keys], q, k, start=True, stop=True).then_inc(at_s, 1)

            def turn(u):
                pe.wait_ge(at_r, u + 1)
                if u >= 2:
                    pe.wait_ge(at_c, u - 1)
                for t in range(UNITS[u][2] + 1):
                    last = pe.transpose(B[2 + u % 2][:, t * P:(t + 1) * P], p_slot(u)[:, t * P:(t + 1) * P], ident[:, :])
                last.then_inc(at_t, 1)

            def heads(g):
                pe.wait_ge(at_c, PER_GROUP * (g + 1))
                if g:
                    pe.wait_ge(at_o, g)
                if g < 2:
                    pe.wait_ge(pj_out, 4 * g + 4)
                first = True
                if g < 4:
                    for h in range(2):
                        for t in range(NT):
                            last = pe.matmul(B[4][:, t * P:T], VB[:, t, 2 * g + h, :],
                                             PT[:, :].rearrange("p (h s q) -> p h s q", h=2, s=NT)[:, h, t, t * P:T],
                                             start=first, stop=h == 1 and t == NT - 1)
                            first = False
                else:
                    for t in range(g - 3):
                        for h in range(2):
                            last = pe.matmul(B[4][:, :], VAP[:, t, h, :], PT[:, (t * 8 + h * 4) * P:(t * 8 + h * 4 + 4) * P],
                                             start=first, stop=h == 1 and t == g - 4)
                            first = False
                last.then_inc(at_v, 1)

            for u in range(-AHEAD, len(UNITS)):
                if u + AHEAD in (0, 16):
                    project((u + AHEAD) // 16)
                if u + AHEAD < len(UNITS):
                    scores(u + AHEAD)
                if u >= 0:
                    turn(u)
                    if u % PER_GROUP == PER_GROUP - 1:
                        heads(u // PER_GROUP)

            pe.wait_ge(at_o, NG)
            pairs(wo_b, KD // 2, XS, xb, KD, m0=M0["wo"])
            norm(norm2, ffn2[0][0])
            ffn(ffn2, norm2, H0["ffn2"], XS, HS, xb, m0=M0["ffn2"])
            norm(norm_final, ffn3[0][0])

            pe.wait_ge(ctx_loaded, 16)
            for t in range(2 * KD):
                if t >= 4:
                    pe.wait_ge(ctx_out, t - 3)
                pe.transpose(B[t % 4][:, 0:P], XIN[:, t // KD, (t % KD) * P:(t % KD + 1) * P], ident[:, :])\
                    .then_inc(ctx_tp, 1)
            norm(norm_x1, None)
            pe.wait_ge(norm_rms, norm_x1.no + 1)
            norm(norm_c1, None)
            ffn(ffn3, norm_c1, H0["ffn3"], XCS, HCS, xcb)
            norm(norm_x2, conv_b)
            pe.wait_ge(norm_rms, norm_x2.no + 1)
            norm(norm_c2, None)
            gate_up(conv_b, KD, XS, xb, (norm_lo, norm_x2.low))
            pairs(bg_b, KD // 2, XS, xb, KD)
            gate_up(gc_b, KD, XS, xb, None, xu=[part(YH, YL, 0, T)], ready_u=(y_split, 0))
            pairs(ga_b, KD // 2, XS, xb, KD)

            def head_sums(b):
                for i in hn_of(b):
                    tok = HN[i][3]
                    pe.wait_ge(hn_sq, i + 1)
                    if i >= 2:
                        pe.wait_ge(hn_rms, i - 1)
                    pe.matmul(B[4 + i % 2][:, 0:tok], ones[:, :], SA[:, i % 2, 0:tok], start=True, stop=True)\
                        .then_inc(hn_mm, 1)

            def head_swaps(b):
                for i in hn_of(b):
                    if HN[i][3] == T:
                        pe.wait_ge(hn_z, i + 1)
                        if i >= 2:
                            pe.wait_ge(hn_out, i - 1)
                        pe.matmul(B[6 + i % 2][:, :], PX[:, :], VA[:, i % 2, 0:T], start=True, stop=True)\
                            .then_inc(hn_sw, 1)

            pe.wait_ge(b_loaded, 32)
            for n in range(HC // 2 + 1):
                b = q_b + n
                s = b % 2
                if b == k_b:
                    pe.wait_ge(w_lo, b + 1)
                    head_sums(b - 1)
                    head_swaps(b - 1)
                    pe.wait_ge(psum_free, b)
                else:
                    begin(b)
                for half in range(2):
                    def wt(k):
                        c = (k * 2 + half) * P
                        return WH[s][:, c:c + P], WL[s][:, c:c + P]
                    if b == k_b:
                        last = tile([(G, U)[half][s][:, :], (G, U)[half][1 - s][:, 0:TC]], wt, XCS, KD,
                                    (norm_lo, norm_c2.low))
                    else:
                        last = tile([(G, U)[half][s][:, :]], wt, XS, KD)
                        if n and half == 0:
                            head_sums(b - 1)
                        if n and half == 1:
                            head_swaps(b - 1)
                last.then_inc(pe_done, 1)
            head_sums(k_b)
            head_swaps(k_b)
            pe.wait_ge(psum_free, v2_b)
            pe.wait_ge(hn_out, len(HN))
            pe.wait_ge(w_lo, v2_b + 1)
            s = v2_b % 2
            for t in range(TK // P):
                if t >= 4:
                    pe.wait_ge(v2_out, t - 3)
                c = (T + t * P) % TK
                for k in range(KD):
                    xh, xl = (z[:, k, c:c + P] for z in (NH, NL))
                    wh, wl = (z[s][:, k * 2 * P:(k + 1) * 2 * P] for z in (WH, WL))
                    o = B[t % 4][:, 0:2 * P]
                    pe.matmul(o, xh, wh, start=k == 0, stop=False)
                    pe.matmul(o, xh, wl, start=False, stop=False)
                    last = pe.matmul(o, xl, wh, start=False, stop=k == KD - 1)
                last.then_inc(v2_mm, 1)
            pe.wait_ge(v2_out, TK // P)
            pe.sem_inc(pe_done, 1)

            def scores2(u):
                g, q, e = UNITS2[u]
                if u >= 2:
                    pe.wait_ge(at2_e, u - 1)
                for k0, k1 in ((0, T), (T, TK)):
                    last = pe.matmul(PS[:, (u % 2) * 1024 + k0:(u % 2) * 1024 + k1],
                                     QT[:, g * 4 + e, q * P:(q + 1) * P], KT[:, g, k0:k1], start=True, stop=True)
                last.then_inc(at2_s, 1)

            def turn2(u):
                pe.wait_ge(at2_r, u + 1)
                for x in range(2):
                    n = 2 * u + x
                    if n >= 3:
                        pe.wait_ge(at2_c, n - 2)
                    for t in range(3):
                        last = pe.transpose(B[4 + n % 3][:, t * P:(t + 1) * P],
                                            p_slot2(u)[:, (3 * x + t) * P:(3 * x + t + 1) * P], ident[:, :])
                    last.then_inc(at2_t, 1)

            def heads2(n):
                pe.wait_ge(at2_c, 8 * (n + 1))
                if n:
                    pe.wait_ge(at2_o, n)
                for t in range(TK // P):
                    last = pe.matmul(B[7][:, :], V2[:, t, (n // NT) * P:(n // NT + 1) * P], PT2[:, t, :, :],
                                     start=t == 0, stop=t == TK // P - 1)
                last.then_inc(at2_v, 1)

            for u in range(-AHEAD, len(UNITS2)):
                if u + AHEAD < len(UNITS2):
                    scores2(u + AHEAD)
                if u >= 0:
                    turn2(u)
                    if u % 4 == 3:
                        heads2(u // 4)
            pe.wait_ge(at2_o, KVC * NT)
            pairs(ba_b, KD // 2, XS, xb, KD)
            pairs(wo2_b, KD // 2, [part(MH, ML, 0, T)], xb, KD, (y_split, KD))
            norm(norm_x3, ffn4[0][0])
            ffn(ffn4, norm_x3, H0["ffn4"], XS, HS, xb, True)
            norm(norm_out, NB)
            pe.wait_ge(norm_x, norm_out.base + KD)
            transposes(lambda t: X[:, t % KD, (t // KD) * P:(t // KD + 1) * P], 1, None)

        @block.scalar
        def _(act):
            def split(s, at, b):
                act.wait_ge(w_loaded[1 - s], at)
                wait(act, pe_done, after(b, 0))
                act.activation(WH[1 - s][:, :], RAW[1 - s][:, :], ACT.Copy).then_inc(w_hi, 1)

            def norm(m):
                for k in range(m.n):
                    act.wait_ge(*m.ready(k))
                    if k >= 2:
                        act.wait_ge(norm_mm, m.base + k - 1)
                    act.activation(SA[:, k % 2, 0:m.tok], m.src(k), ACT.Square).then_inc(norm_sq, 1)
                act.wait_ge(norm_mm, m.base + m.n)
                act.activation(RB[:, 0:m.tok], B[7][:, 0:m.tok], ACT.Sqrt, bias=eps[:, :],
                               scale=1.0 / (m.n * P)).then_inc(norm_rms, 1)
                if m.dst:
                    for k in range(m.n):
                        act.wait_ge(norm_x, m.base + k + 1)
                        act.activation(m.dst(k)[0], VA[:, k % 2, 0:m.tok], ACT.Copy).then_inc(norm_hi, 1)

            def mods(b0, j, s, m0):
                if m0 is None:
                    return
                t = (s + b0) % 2
                act.wait_ge(mod_done, j + (m0 + 1))
                nv = vectors(m0)
                act.activation(MOD[:, ds(j + m0, 1), 0:nv].rearrange("p a b -> p (a b)"), B[4 + t][:, 0:nv], ACT.Copy)\
                    .then_inc(mod_out, 1)

            def gate_up(b0, n, tok, m0=None, func=ACT.Silu):
                for b, j, s, at in stage(act, b0, n):
                    split(s, at, b)
                    act.wait_ge(pe_done, b + 1)
                    wait(act, psum_free, after(b, -1))
                    if tok > T:
                        act.activation(SA[:, s, T:tok], CG[s][:, 0:tok - T], func)
                    act.activation(SA[:, s, 0:T], G[s][:, :], func).then_inc(gate_done, 1)
                    mods(b0, j, s, m0)

            def only_split(b0, n, straight=False, m0=None):
                for b, j, s, at in stage(act, b0, n, straight):
                    if at is not None:
                        split(s, at, b)
                    mods(b0, j, s, m0)

            def ffn(stages, tok, last=False, m0=None):
                for c, (kn, (bg, bd)) in enumerate(zip(CHUNKS, stages)):
                    gate_up(bg, kn, tok, m0)
                    m1 = None if m0 is None else m0 + kn
                    only_split(bd, KD // 2, last and c == 2, m1)
                    m0 = None if m0 is None else m1 + KD // 2

            act.wait_ge(w_loaded[0], loaded(0, 0))
            act.activation(WH[0][:, :], RAW[0][:, :], ACT.Copy).then_inc(w_hi, 1)
            act.wait_ge(c2_s, 2)
            act.wait_ge(c_loaded, 32)
            for v, name in enumerate(("c", "c_ctx")):
                last = act.activation(CV2[:, :, v], vecs[:, VEC[name][0]:VEC[name][0] + KD], ACT.Silu)
            last.then_inc(act_s, 1)
            norm(norm1)
            ffn(ffn1, T, m0=M0["ffn1"])
            norm(norm_mix)
            for n in range(10):
                b = w_in_b + n
                split(b % 2, loaded(b, 1), b)
                for i, half in enumerate(COPIED[n], COPY0[n]):
                    if i == COPY0[n]:
                        act.wait_ge(pe_done, b + 1)
                    if i >= 2:
                        done = [ITEM0[m] + len([x for x in ITEMS[m] if x[1] <= h]) for m in range(10) for h in COPIED[m]]
                        act.wait_ge(rope_mm, done[i - 2])
                    act.activation(SA[:, i % 2, 0:T], (G, U)[half][b % 2][:, :], ACT.Copy).then_inc(rope_y, 1)
            norm(norm_q)
            norm(norm_kv)
            n = 0
            for q in range(1, NT):
                for h in range(IDX_HEADS):
                    act.wait_ge(ix_mm, n + 1)
                    if n >= 2:
                        act.wait_ge(ix_acc, n - 1)
                    act.activation(SA[:, n % 2, 0:(q + 1) * P], B[n % 2][:, 0:(q + 1) * P], ACT.Relu).then_inc(ix_relu, 1)
                    n += 1
            split(v_b % 2, loaded(v_b, 1), v_b)

            def project(n):
                b = pj_b + n
                split(b % 2, loaded(b, 1), b)
                for i in range(4):
                    act.wait_ge(pj_mm, 4 * n + i + 1)
                    if 4 * n + i >= 2:
                        act.wait_ge(pj_sw, 4 * n + i - 1)
                    act.activation(SF[0:96, (i % 2) * T:(i % 2 + 1) * T], B[6][0:96, :], ACT.Copy).then_inc(pj_y, 1)

            def exp(u):
                act.wait_ge(at_m, u + 1)
                keys = (UNITS[u][2] + 1) * P
                p = p_slot(u)[:, 0:keys]
                act.activation(p, p, ACT.Exp, bias=stat(NM, u), accum_out=stat(DEN, u))\
                    .then_inc(at_e, 1)

            def turned(u):
                g = u // PER_GROUP
                act.wait_ge(at_t, u + 1)
                if u % PER_GROUP == 0 and g:
                    act.wait_ge(at_v, g)
                keys = (UNITS[u][2] + 1) * P
                act.activation(pt_of(u), B[2 + u % 2][:, 0:keys].rearrange("p (s q) -> p s q", q=P), ACT.Copy)\
                    .then_inc(at_c, 1)

            def heads(g):
                act.wait_ge(at_v, g + 1)
                o = heads_out(g, NH)
                i = B[4][:, :] if g < 4 else B[4][:, :].rearrange("p (h q) -> p h q", h=4)
                act.activation(o, i, ACT.Copy).then_inc(at_h, 1)

            for u in range(-AHEAD, len(UNITS)):
                if u + AHEAD in (0, 16):
                    project((u + AHEAD) // 16)
                if 0 <= u + AHEAD - 1 < len(UNITS):
                    exp(u + AHEAD - 1)
                if u >= 0:
                    if u % PER_GROUP == 0 and u:
                        heads(u // PER_GROUP - 1)
                    turned(u)
            heads(NG - 1)
            only_split(wo_b, KD // 2, m0=M0["wo"])
            norm(norm2)
            ffn(ffn2, T, m0=M0["ffn2"])
            norm(norm_final)

            norm(norm_x1)
            norm(norm_c1)
            ffn(ffn3, T + TC)
            norm(norm_x2)
            norm(norm_c2)
            gate_up(conv_b, KD, T, func=ACT.Copy)
            only_split(bg_b, KD // 2)
            gate_up(gc_b, KD, T, func=ACT.Sigmoid)
            for b, j, s, at in stage(act, ga_b, KD // 2):
                split(s, at, b)
                act.wait_ge(pe_done, b + 1)
                for half in range(2):
                    o = GA[:, ds(j * 2 + half, 1), :].rearrange("p a t -> p (a t)")
                    last = act.activation(o, (G, U)[half][s][:, :], ACT.Sigmoid)
                last.then_inc(ga_done, 1)
            for b in range(q_b, k_b + 1):
                split(b % 2, loaded(b, 1), b)
                act.wait_ge(pe_done, b + 1)
                for wave in hn_waves(b):
                    for i in wave:
                        tok = HN[i][3]
                        if i >= 2:
                            act.wait_ge(hn_z, i - 1)
                        act.activation(SA[:, i % 2, 0:tok], hn_bank(i), ACT.Square).then_inc(hn_sq, 1)
                    for i in wave:
                        tok = HN[i][3]
                        act.wait_ge(hn_mm, i + 1)
                        act.activation(SA[:, i % 2, 0:tok], B[4 + i % 2][:, 0:tok], ACT.Sqrt, bias=eps[:, :],
                                       scale=1.0 / P).then_inc(hn_rms, 1)
            split(v2_b % 2, loaded(v2_b, 1), v2_b)

            def exp2(u):
                act.wait_ge(at2_m, u + 1)
                if u >= 4:
                    act.wait_ge(at2_t, 2 * (u - 3))
                act.activation(p_slot2(u), PS[:, (u % 2) * 1024:(u % 2) * 1024 + TK], ACT.Exp,
                               bias=stat(NM, u), scale=float(P) ** -0.5, accum_out=stat(DEN, u)).then_inc(at2_e, 1)

            def turned2(u):
                n = u // 4
                for x in range(2):
                    act.wait_ge(at2_t, 2 * u + x + 1)
                    if u % 4 == 0 and x == 0 and n:
                        act.wait_ge(at2_v, n)
                    act.activation(PT2[:, 3 * x:3 * x + 3, u % 4, :],
                                   B[4 + (2 * u + x) % 3][:, 0:3 * P].rearrange("p (t q) -> p t q", q=P),
                                   ACT.Copy).then_inc(at2_c, 1)

            def heads2(n):
                act.wait_ge(at2_v, n + 1)
                g, q = n // NT, n % NT
                act.activation(NH[:, g * 4:g * 4 + 4, q * P:(q + 1) * P],
                               B[7][:, :].rearrange("p (h q) -> p h q", h=4), ACT.Copy).then_inc(at2_h, 1)

            for u in range(1 - AHEAD, len(UNITS2)):
                if u + AHEAD - 1 < len(UNITS2):
                    exp2(u + AHEAD - 1)
                if u >= 0:
                    if u % 4 == 0 and u:
                        heads2(u // 4 - 1)
                    turned2(u)
            heads2(len(UNITS2) // 4 - 1)
            only_split(ba_b, KD // 2)
            only_split(wo2_b, KD // 2)
            norm(norm_x3)
            ffn(ffn4, T, True)
            norm(norm_out)

        @block.vector
        def _(dve):
            own = Count(dve_s)

            def split(s, b):
                dve.wait_ge(w_hi, b + 2)
                dve.tensor_tensor(WL[1 - s][:, :], RAW[1 - s][:, :], WH[1 - s][:, :].bitcast(F32),
                                  ALU.subtract).then_inc(w_lo, 1)

            def norm(m):
                dve.wait_ge(norm_rms, m.no + 1)
                own.settle(dve, dve.reciprocal(RB[:, 0:m.tok], RB[:, 0:m.tok]))

                def low(k):
                    dve.wait_ge(norm_hi, m.low + k + 1)
                    h, l = m.dst(k)
                    dve.tensor_tensor(l, VA[:, k % 2, 0:m.tok], h.bitcast(F32), ALU.subtract).then_inc(norm_lo, 1)

                for k in range(m.n):
                    if m.dst and k >= 2:
                        dve.wait_ge(norm_lo, m.low + k - 1)
                    o = VA[:, k % 2, 0:m.tok] if m.dst else m.src(k)
                    ins = dve.scalar_tensor_tensor(out=o, in0=m.src(k), scalar=m.gain(k), in1=RB[:, 0:m.tok],
                                                   op0=ALU.mult, op1=ALU.mult)
                    if m.shift:
                        own.settle(dve, ins)
                        ins = dve.tensor_scalar(o, o, m.shift(k), None, ALU.add)
                    ins.then_inc(norm_x, 1)
                    if m.dst and k:
                        low(k - 1)
                if m.dst:
                    low(m.n - 1)

            def mods(b0, j, s, m0):
                if m0 is None:
                    return
                t = (s + b0) % 2
                dve.wait_ge(mod_loaded[t], j * 8 + (8 * (m0 - t) + 16))
                wait(dve, mod_done, after(j + m0, -1))
                for k in range(KD):
                    if k:
                        dve.wait_ge(mod_s, j * KD + (KD * m0 + k))
                    for v in range(vectors(m0)):
                        o = MACC[:, t, v, :]
                        if k:
                            last = dve.scalar_tensor_tensor(out=o, in0=MW[t][:, k, :], scalar=CV2[:, k, v:v + 1],
                                                            in1=o, op0=ALU.mult, op1=ALU.add)
                        else:
                            last = dve.tensor_scalar(o, MW[t][:, k, :], CV2[:, k, v:v + 1], None, ALU.mult)
                    last.then_inc(mod_s, 1)

            def gate_up(b0, n, tok, g0, h0, m0=None):
                for b, j, s, at in stage(dve, b0, n):
                    mods(b0, j, s, m0)
                    split(s, b)
                    dve.wait_ge(gate_done, j + (g0 + 1))
                    wait(dve, h_split, after(j + h0, -1))
                    if tok > T:
                        dve.tensor_tensor(VA[:, s, T:tok], SA[:, s, T:tok], CU[s][:, 0:tok - T], ALU.mult)
                    dve.tensor_tensor(VA[:, s, 0:T], SA[:, s, 0:T], U[s][:, :], ALU.mult).then_inc(psum_free, 1)

            def down(b0, tok, by, by_ctx, straight=False, m0=None):
                for b, j, s, at in stage(dve, b0, KD // 2, straight):
                    mods(b0, j, s, m0)
                    if at is not None:
                        split(s, b)
                    dve.wait_ge(pe_done, b + 1)
                    dve.wait_ge(psum_free, b)
                    for half, bank in enumerate((G, U)):
                        if tok > T:
                            o = CX[:, ds(j * 2 + half, 1), :].rearrange("p a t -> p (a t)")
                            dve.scalar_tensor_tensor(out=o, in0=(CG, CU)[half][s][:, 0:tok - T],
                                                     scalar=by_ctx(j * 2 + half), in1=o, op0=ALU.mult, op1=ALU.add)
                        o = X[:, ds(j * 2 + half, 1), :].rearrange("p a t -> p (a t)")
                        last = dve.scalar_tensor_tensor(out=o, in0=bank[s][:, :], scalar=by(j * 2 + half), in1=o,
                                                        op0=ALU.mult, op1=ALU.add)
                    last.then_inc(psum_free, 1)

            def ffn(stages, tok, name, by, by_ctx=None, last=False):
                g0, h0, m0 = G0[name], H0[name], M0.get(name)
                for c, (kn, (bg, bd)) in enumerate(zip(CHUNKS, stages)):
                    gate_up(bg, kn, tok, g0, h0, m0)
                    m1 = None if m0 is None else m0 + kn
                    down(bd, tok, by, by_ctx, last and c == 2, m1)
                    m0 = None if m0 is None else m1 + KD // 2
                    g0, h0 = g0 + kn, h0 + kn

            def transposed(no, dst_of):
                for t in range(32):
                    dve.wait_ge(tp_done, no * 32 + t + 1)
                    dve.tensor_copy(dst_of(t), B[t % 4][:, 0:P]).then_inc(tp_out, 1)

            dve.memset(ones[:, :], 1.0).then_inc(c2_s, 1)
            dve.wait_ge(c2_s, 1)
            dve.memset(eps[:, :], EPS).then_inc(c2_s, 1)
            dve.wait_ge(c_loaded, 32)
            dve.wait_ge(w_hi, 1)
            dve.tensor_tensor(WL[0][:, :], RAW[0][:, :], WH[0][:, :].bitcast(F32), ALU.subtract).then_inc(w_lo, 1)
            transposed(0, lambda t: X[:, t % KD, (t // KD) * P:(t // KD + 1) * P])
            norm(norm1)
            dve.wait_ge(act_s, 1)
            ffn(ffn1, T, "ffn1", lambda t: 0.5)
            norm(norm_mix)
            dve.wait_ge(a_loaded, 64)
            own.settle(dve, dve.memset(VAP[:, :, :, :], 0.0))
            for n in range(10):
                b = w_in_b + n
                s = b % 2
                split(s, b)
                dve.wait_ge(pe_done, b + 1)
                for i, half in enumerate(COPIED[n], COPY0[n]):
                    dve.wait_ge(rope_y, i + 1)
                for kind, half, _ in ITEMS[n]:
                    y = (G, U)[half][s]
                    if kind == "rope":
                        own.settle(dve, dve.tensor_tensor(VA[:, half, 0:T], y[:, :], TA[:, 0, :], ALU.mult))
                    if kind == "kr":
                        own.settle(dve, dve.tensor_tensor(KPE[64:96, :], y[64:96, :], TB[64:96, 0, :], ALU.mult))
                for half, t in enumerate(W_IN_TILES[2 * n:2 * n + 2]):
                    if t[0] == "lat":
                        own.settle(dve, dve.tensor_copy(CQ[:, t[1], :], (G, U)[half][s][:, :]))
                        dve.sem_inc(lat_out, 1)
                dve.sem_inc(psum_free, 1)
                for i, (kind, half, dst) in enumerate(ITEMS[n], ITEM0[n]):
                    dve.wait_ge(rope_mm, i + 1)
                    o = B[4 + i % 2]
                    if kind in ("wi", "va"):
                        turned = o[:, :].rearrange("p (t c) -> p t c", c=P)
                    if kind == "wi":
                        ins = dve.tensor_scalar(WI[:, :, :], turned[:, :, 96:96 + IDX_HEADS],
                                                float(IDX_HEADS * 64) ** -0.5, None, ALU.mult)
                    elif kind == "va":
                        dve.tensor_copy(VAP[:, :, 0, 0:64], turned[:, :, 64:128])
                        ins = dve.tensor_copy(VAP[:, :, 1, 64:128], turned[:, :, 64:128])
                    else:
                        r, tab = (slice(64, 96), TB) if kind == "kr" else (slice(0, P), TA)
                        if kind == "twice":
                            own.settle(dve, dve.tensor_tensor(VA[:, half, 0:T], B[6 + i % 2][:, :], TA[:, 0, :], ALU.mult))
                        own.settle(dve, dve.tensor_tensor(RB[r, :], o[r, :], tab[r, 1, :], ALU.mult))
                        a, d = (KPE[r, :], KPE[r, :]) if kind == "kr" else (VA[r, half, 0:T], dst)
                        ins = dve.tensor_tensor(d, a, RB[r, :], ALU.add)
                    ins.then_inc(rope_out, 1)
                    dve.wait_ge(rope_out, i + 1)
            norm(norm_q)
            norm(norm_kv)

            n = 0
            for q in range(1, NT):
                keys = (q + 1) * P
                acc = BIAS[:, q - 1, 0:keys]
                for h in range(IDX_HEADS):
                    dve.wait_ge(ix_relu, n + 1)
                    if n:
                        dve.wait_ge(ix_acc, n)
                    dve.scalar_tensor_tensor(out=acc, in0=SA[:, n % 2, 0:keys], scalar=WI[:, q, h:h + 1],
                                             in1=acc if h else CM[:, (NT - 1 - q) * P:T],
                                             op0=ALU.mult, op1=ALU.add).then_inc(ix_acc, 1)
                    n += 1

            def select():
                for q in range(1, NT):
                    acc = BIAS[:, q - 1, 0:(q + 1) * P]
                    for r in range(TOPK // 8):
                        own.settle(dve, dve.max(M8[:, :], acc))
                        own.settle(dve, dve.match_replace(acc, M8[:, :], acc, 3 * NEG * 1e7))
                        yield
                    own.settle(dve, dve.tensor_scalar(acc, acc, 2 * NEG * 1e7, NEG, ALU.is_gt, ALU.mult))

            split(v_b % 2, v_b)
            dve.wait_ge(ix_acc, n)
            dve.wait_ge(v_zero, 1)
            for t in range(NT):
                dve.wait_ge(v_mm, t + 1)
                v = B[2 + t % 2][:, :].rearrange("p (h b c) -> p h b c", h=4, b=2)
                o = VB[:, t, :, :].rearrange("p (h b) c -> p h b c", b=2)
                dve.tensor_copy(o[:, :, 0, 0:64], v[:, :, 0, :])
                dve.tensor_copy(o[:, :, 1, 64:128], v[:, :, 1, :]).then_inc(v_out, 1)
            dve.wait_ge(v_out, NT)
            dve.sem_inc(psum_free, 1)
            for i in range(4):
                own.settle(dve, dve.tensor_copy(KB[64:96, i, :], KPE[64:96, :]))

            def project(n):
                b = pj_b + n
                split(b % 2, b)
                for i in range(4):
                    dve.wait_ge(pj_mm, 4 * n + i + 1)
                    dve.wait_ge(pj_y, 4 * n + i + 1)
                    own.settle(dve, dve.tensor_tensor(RB[0:96, :], B[6][0:96, :], TB[0:96, 0, :], ALU.mult))
                    dve.tensor_copy(KB[0:64, i, :], B[7][0:64, :])
                    dve.wait_ge(pj_sw, 4 * n + i + 1)
                    own.settle(dve, dve.tensor_tensor(QB[0:96, i, :], B[4][0:96, :], TB[0:96, 1, :], ALU.mult))
                    dve.tensor_tensor(QB[0:96, i, :], QB[0:96, i, :], RB[0:96, :], ALU.add).then_inc(pj_out, 1)
                    dve.wait_ge(pj_out, 4 * n + i + 1)
                dve.sem_inc(psum_free, 1)

            def masked(u):
                kind, h, q = UNITS[u]
                keys = (q + 1) * P
                dve.wait_ge(at_s, u + 1)
                if u >= 4:
                    dve.wait_ge(at_t, u - 3)
                bias = CM[:, (NT - 1 - q) * P:T] if kind == "b" or q == 0 else BIAS[:, q - 1, 0:keys]
                scale = float(96 if kind == "b" else 64) ** -0.5
                nm = stat(NM, u)
                own.settle(dve, dve.tensor_tensor_reduce(out=p_slot(u)[:, 0:keys], in0=B[u % 2][:, 0:keys], in1=bias,
                                                         scale=scale, scalar=3 * NEG * 1e7, op0=ALU.add, op1=ALU.max,
                                                         accum_out=nm))
                dve.tensor_scalar(nm, nm, -1.0, None, ALU.mult).then_inc(at_m, 1)

            def normalised(u):
                keys = (UNITS[u][2] + 1) * P
                d = stat(DEN, u)
                dve.wait_ge(at_e, u + 1)
                own.settle(dve, dve.reciprocal(d, d))
                p = p_slot(u)[:, 0:keys]
                dve.tensor_scalar(p, p, d, None, ALU.mult).then_inc(at_r, 1)

            def heads(g):
                dve.wait_ge(at_h, g + 1)
                i = B[4][:, :] if g < 4 else B[4][:, :].rearrange("p (h q) -> p h q", h=4)
                dve.tensor_tensor(heads_out(g, NL), i, heads_out(g, NH).bitcast(F32), ALU.subtract).then_inc(at_o, 1)

            selection = select()
            for u in range(-AHEAD, len(UNITS)):
                if u >= 0:
                    normalised(u)
                if u + AHEAD in (0, 16):
                    project((u + AHEAD) // 16)
                if u + AHEAD == 32:
                    for _ in selection:
                        pass
                if u + AHEAD < len(UNITS):
                    masked(u + AHEAD)
                if u >= 0:
                    if u % PER_GROUP == 1 and u > 1:
                        heads(u // PER_GROUP - 1)
                    if u < 32:
                        next(selection, None)
                        if u % 2:
                            next(selection, None)
            heads(NG - 1)
            down(wo_b, T, lambda t: 1.0, None, m0=M0["wo"])
            norm(norm2)
            ffn(ffn2, T, "ffn2", lambda t: 0.5)
            dve.wait_ge(mod_out, NMOD * KD)
            c = VEC["b_mod"][0]
            for v, n in enumerate((NMOD * KD, NCTX)):
                own.settle(dve, dve.tensor_tensor(MOD[:, 0:n, v], MOD[:, 0:n, v], vecs[:, c:c + n], ALU.add))
            for n, (name, i, v) in enumerate(MODULATED):
                own.inc(dve.scalar_tensor_tensor(out=GS[:, n, :], in0=MOD[:, i * KD:(i + 1) * KD, v], scalar=1.0,
                                                 in1=vecs[:, VEC[name][0]:VEC[name][0] + KD], op0=ALU.add,
                                                 op1=ALU.mult))
            for n, (i, v) in enumerate(HALVED):
                own.settle(dve, dve.tensor_scalar(HG[:, n, :], MOD[:, i * KD:(i + 1) * KD, v], 0.5, None, ALU.mult))
            norm(norm_final)

            for t in range(2 * KD):
                dve.wait_ge(ctx_tp, t + 1)
                dve.tensor_copy(CX[:, t % KD, (t // KD) * P:(t // KD + 1) * P], B[t % 4][:, 0:P]).then_inc(ctx_out, 1)
            dve.wait_ge(norm_x, norm_final.base + KD)
            norm(norm_x1)
            norm(norm_c1)
            ffn(ffn3, T + TC, "ffn3", lambda t: HG[:, 0, ds(t, 1)], lambda t: HG[:, 1, ds(t, 1)])
            norm(norm_x2)
            norm(norm_c2)
            dve.wait_ge(norm_lo, norm_c2.low + KD)
            dve.memset(VA[:, :, 0:T + 2], 0.0).then_inc(conv_s, 1)
            for b, j, s, at in stage(dve, conv_b, KD):
                split(s, b)
                dve.wait_ge(gate_done, j + (G0["conv"] + 1))
                dve.wait_ge(conv_s, j * 3 + 1)
                dve.tensor_tensor(VA[:, s, 1:T + 1], SA[:, s, 0:T], U[s][:, :], ALU.mult).then_inc(psum_free, 1)
                dve.wait_ge(psum_free, b + 1)
                o = M[:, ds(j, 1), :].rearrange("p a t -> p (a t)")
                for tap in range(3):
                    w = vecs[:, ds(j + (VEC["conv"][0] + tap * KD), 1)]
                    src = VA[:, s, tap:tap + T]
                    if tap == 0:
                        dve.tensor_scalar(o, src, w, None, ALU.mult).then_inc(conv_s, 1)
                    else:
                        dve.wait_ge(conv_s, j * 3 + (tap + 1))
                        dve.scalar_tensor_tensor(out=o, in0=src, scalar=w, in1=o, op0=ALU.mult, op1=ALU.add)\
                            .then_inc(conv_s, 1)
            dve.wait_ge(conv_s, 3 * KD + 1)
            for b, j, s, at in stage(dve, bg_b, KD // 2, True):
                split(s, b)
                dve.wait_ge(pe_done, b + 1)
                if j:
                    dve.wait_ge(y_split, 2 * j)
                for half in range(2):
                    last = dve.tensor_tensor(VA[:, half, 0:T], (G, U)[half][s][:, :], M[:, 2 * j + half, :], ALU.mult)
                last.then_inc(psum_free, 1)
            dve.wait_ge(psum_free, gc_b)
            for b, j, s, at in stage(dve, gc_b, KD):
                split(s, b)
                dve.wait_ge(gate_done, j + (G0["gc"] + 1))
                dve.wait_ge(pe_done, b + 1)
                dve.tensor_tensor(M[:, ds(j, 1), :].rearrange("p a t -> p (a t)"), SA[:, s, 0:T], U[s][:, :],
                                  ALU.mult).then_inc(psum_free, 1)
            for b, j, s, at in stage(dve, ga_b, KD // 2):
                split(s, b)
                dve.wait_ge(ga_done, j + 1)
                dve.sem_inc(psum_free, 1)
            dve.wait_ge(b_loaded, 32)
            for b in range(q_b, k_b + 1):
                split(b % 2, b)
                for wave in hn_waves(b):
                    for i in wave:
                        tok = HN[i][3]
                        dve.wait_ge(hn_rms, i + 1)
                        own.settle(dve, dve.reciprocal(SA[:, i % 2, 0:tok], SA[:, i % 2, 0:tok]))
                        if i >= 2:
                            dve.wait_ge(hn_out, i - 1)
                        o = VA[:, i % 2, 0:tok] if tok == T else HN[i][5]
                        dve.scalar_tensor_tensor(out=o, in0=hn_bank(i), scalar=vec(HN[i][4]), in1=SA[:, i % 2, 0:tok],
                                                 op0=ALU.mult, op1=ALU.mult).then_inc(hn_z, 1)
                    dve.wait_ge(hn_z, i + 1)
                    if wave[-1] == hn_of(b)[-1]:
                        dve.sem_inc(psum_free, 1)
                    for i in wave:
                        if HN[i][3] == T:
                            own.settle(dve, dve.tensor_tensor(RB[:, :], VA[:, i % 2, 0:T], TX[:, 0, :], ALU.mult))
                            dve.wait_ge(hn_sw, i + 1)
                            own.settle(dve, dve.tensor_tensor(HN[i][5], B[6 + i % 2], TX[:, 1, :], ALU.mult))
                            own.settle(dve, dve.tensor_tensor(HN[i][5], HN[i][5], RB[:, :], ALU.add))
                        dve.sem_inc(hn_out, 1)
            split(v2_b % 2, v2_b)
            for t in range(TK // P):
                dve.wait_ge(v2_mm, t + 1)
                dve.tensor_copy(V2[:, t, :], B[t % 4][:, 0:2 * P]).then_inc(v2_out, 1)
            dve.wait_ge(v2_out, TK // P)
            dve.sem_inc(psum_free, 1)

            def maximum2(u):
                dve.wait_ge(at2_s, u + 1)
                if u >= 4:
                    dve.wait_ge(at2_e, u - 3)
                nm = stat(NM, u)
                own.settle(dve, dve.tensor_reduce(nm, PS[:, (u % 2) * 1024:(u % 2) * 1024 + TK], AX.X, ALU.max,
                                                  negate=True))
                dve.tensor_scalar(nm, nm, float(P) ** -0.5, None, ALU.mult).then_inc(at2_m, 1)

            def normalised2(u):
                d = stat(DEN, u)
                dve.wait_ge(at2_e, u + 1)
                own.settle(dve, dve.reciprocal(d, d))
                p = p_slot2(u)
                dve.tensor_scalar(p, p, d, None, ALU.mult).then_inc(at2_r, 1)

            def heads2(n):
                dve.wait_ge(at2_h, n + 1)
                g, q = n // NT, n % NT
                h, l = (z[:, g * 4:g * 4 + 4, q * P:(q + 1) * P] for z in (NH, NL))
                dve.tensor_tensor(l, B[7][:, :].rearrange("p (h q) -> p h q", h=4), h.bitcast(F32), ALU.subtract)\
                    .then_inc(at2_o, 1)

            for u in range(-AHEAD, len(UNITS2)):
                if u >= 0:
                    normalised2(u)
                if u + AHEAD < len(UNITS2):
                    maximum2(u + AHEAD)
                if u % 4 == 1 and u > 1:
                    heads2(u // 4 - 1)
            heads2(len(UNITS2) // 4 - 1)
            for b, j, s, at in stage(dve, ba_b, KD // 2, True):
                split(s, b)
                dve.wait_ge(pe_done, b + 1)
                if j:
                    dve.wait_ge(y_split, KD + 2 * j)
                for half in range(2):
                    own.inc(dve.tensor_tensor(VA[:, half, 0:T], (G, U)[half][s][:, :], GA[:, 2 * j + half, :], ALU.mult))
                for half in range(2):
                    dve.wait_ge(dve_s, own.n)
                    last = dve.tensor_tensor(VA[:, half, 0:T], VA[:, half, 0:T], M[:, 2 * j + half, :], ALU.add)
                last.then_inc(psum_free, 1)
            down(wo2_b, T, lambda t: mod(5, t, 0), None)
            norm(norm_x3)
            ffn(ffn4, T, "ffn4", lambda t: HG[:, 2, ds(t, 1)], None, True)
            norm(norm_out)
            transposed(1, lambda t: XIN[:, t // KD, (t % KD) * P:(t % KD + 1) * P])

        @block.gpsimd
        def _(pool):
            def hidden(b0, n, tok, g0):
                for b, j, s, _ in stage(pool, b0, n):
                    pool.wait_ge(psum_free, b + 1)
                    h = HH[:, ds(j, 1), 0:tok].rearrange("p a t -> p (a t)")
                    l = HL[:, ds(j, 1), 0:tok].rearrange("p a t -> p (a t)")
                    pool.tensor_copy(h, VA[:, s, 0:tok]).then_inc(pool_s, 1)
                    pool.wait_ge(pool_s, j + (g0 + 1))
                    pool.tensor_tensor(l, VA[:, s, 0:tok], h.bitcast(F32), ALU.subtract).then_inc(h_split, 1)

            def ffn(stages, tok, g0):
                for kn, (bg, bd) in zip(CHUNKS, stages):
                    hidden(bg, kn, tok, g0)
                    g0 += kn

            def branch(b0, h_to, l_to, y0):
                for b, j, s, _ in stage(pool, b0, KD // 2, True):
                    pool.wait_ge(psum_free, b + 1)
                    for half in range(2):
                        t = 2 * j + half
                        pool.tensor_copy(h_to[:, t, :], VA[:, half, 0:T]).then_inc(y_part, 1)
                        pool.wait_ge(y_part, y0 + t + 1)
                        pool.tensor_tensor(l_to[:, t, :], VA[:, half, 0:T], h_to[:, t, :].bitcast(F32), ALU.subtract)\
                            .then_inc(y_split, 1)

            ffn(ffn1, T, 0)
            pool.wait_ge(ix_acc, 3 * IDX_HEADS)
            pool.memset(VB[:, :, :, :], 0.0).then_inc(v_zero, 1)
            ffn(ffn2, T, H0["ffn2"])
            ffn(ffn3, T + TC, H0["ffn3"])
            branch(bg_b, YH, YL, 0)
            branch(ba_b, MH, ML, KD)
            ffn(ffn4, T, H0["ffn4"])


def _vectors(inputs):
    import numpy as np
    named = {"g_ffn1": "g_ffn1", "g_mix": "g_mix", "g_ffn2": "g_ffn2", "g_final": "g_final", "g_q_lat": "g_q_lat",
             "g_kv_lat": "g_kv_lat", "norm1": "norm1_g_2", "norm2": "norm2_g_2", "norm3": "norm3_g_2",
             "final": "final_g_2", "q_norm": "q_norm_g_2", "k_norm": "k_norm_g_2", "b_mod": "b_mod_2",
             "conv": "conv_w_2", "c": "c_2", "c_ctx": "c_ctx_2"}
    return np.ascontiguousarray(np.concatenate(
        [np.asarray(inputs[named[n]]).reshape(-1, P).T for n in VEC], axis=1))


def _constants():
    import numpy as np
    f32 = np.float32

    def rope(dim):
        inv = f32(10000.0) ** (-np.arange(0, dim, 2, dtype=f32) / f32(dim))
        ang = (np.arange(T, dtype=f32)[:, None] * inv[None, :]).T
        return np.cos(ang), np.sin(ang)

    c, s = rope(64)
    rope64 = np.stack([np.tile(c, (4, 1)), np.concatenate([-s, s, -s, s])], 1)
    c, s = rope(32)
    rope96 = np.zeros((P, 2, T), f32)
    rope96[:64, 0] = 1.0
    rope96[64:96, 0] = np.concatenate([c, c])
    rope96[64:96, 1] = np.concatenate([-s, s])
    perms = np.zeros((P, 4, P), f32)
    for r in range(P):
        perms[r ^ 32, 0, r] = 1
        perms[r % 64, 1, r] = 1
        perms[(r % 64) ^ 32, 2, r] = 1
    for r in range(64, 96):
        perms[r ^ 16, 3, r] = 1
    inv = f32(10000.0) ** (-np.arange(32, dtype=f32) / f32(32))
    t = np.arange(T)
    ang = [(z.astype(f32)[:, None] * inv).T for z in (t // 64, t % 64)]
    rope128 = np.stack([np.concatenate([np.cos(a) for a in ang for _ in range(2)]),
                        np.concatenate([f(np.sin(a)) for a in ang for f in (np.negative, np.positive)])], 1)
    q, k = np.arange(P)[:, None], np.arange(P)[None, :]
    causal = np.zeros((P, T), f32)
    causal[:, T - P:] = np.where(k <= q, 0.0, NEG)
    return {"ident": np.eye(P, dtype=f32), "rope64": rope64.astype(f32), "rope96": rope96, "perms": perms,
            "causal": causal, "rope128": rope128.astype(f32)}


_WEIGHTS = ["x", "w1_gate", "w1_up", "w1_down", "w_in", "w_uq", "w_ukv", "w_out", "w2_gate", "w2_up", "w2_down",
            "ctx_2", "w_mod_2", "ffn1_w_in_2", "ffn1_w_out_2", "w_in_2", "w_branch_conv_2", "w_branch_attn_2", "w_out_2",
            "ffn2_w_in_2", "ffn2_w_out_2"]
_OUT = (1, 512, 1024)


def kernel(**inputs):
    import numpy as np
    import concourse.bacc as bacc
    from concourse.bass_utils import run_bass_kernel_spmd

    nc = bacc.Bacc("TRN2", target_bir_lowering=False, num_devices=1)
    given = {n: np.ascontiguousarray(inputs[n]) for n in _WEIGHTS}
    given["vecs"] = _vectors(inputs)
    given.update(_constants())
    arrays, aps = {}, {}
    for name, a in given.items():
        arrays[f"in_{name}"] = a
        aps[name] = nc.dram_tensor(f"in_{name}", a.shape, mybir.dt.from_np(a.dtype), kind="ExternalInput").ap()
    out = nc.dram_tensor("out_0", _OUT, F32, kind="ExternalOutput").ap()
    build(nc, aps, out)
    r = run_bass_kernel_spmd(nc, [arrays], core_ids=[0])
    return r.results[0]["out_0"]
```

```python
import concourse.bass as bass
from concourse import mybir
from contextlib import ExitStack

P = 128
F32 = mybir.dt.float32
F32R = mybir.dt.float32r
ACT = mybir.ActivationFunctionType
ALU = mybir.AluOpType
AX = mybir.AxisListType
ds = bass.ds

T, TC, D, DFF = 512, 256, 1024, 2816
KD = D // P
CHUNKS = (8, 8, 6)
HMAX = max(CHUNKS)
SLOT = 16 * P
EPS = 1e-6
NMOD = 9
NEG = -1e30
NT = T // P
HA, HB = 8, 8
HC, KVC, TK = 8, 2, T + TC
IDX_HEADS, TOPK = 16, 128
W_IN_TILES = ([("qi", j, 640 + j * P) for j in range(8)] + [("misc", 0, None), ("kv", 0, 512)]
              + [("qa", j, j * P) for j in range(4)] + [("lat", j, 1744 + j * P) for j in range(5)])
MISC = ((1664, 64, 0), (2384, 32, 64), (1728, 16, 96))
assert sum(CHUNKS) * P == DFF

VEC = {}
_at = 0
for _name, _n in (("g_ffn1", 8), ("g_mix", 8), ("g_ffn2", 8), ("g_final", 8), ("g_q_lat", 3), ("g_kv_lat", 2),
                  ("norm1", 8), ("norm2", 8), ("norm3", 8), ("final", 8), ("q_norm", 1), ("k_norm", 1),
                  ("b_mod", NMOD * KD), ("conv", 24), ("c", 8), ("c_ctx", 8)):
    VEC[_name] = (_at, _n)
    _at += _n
NVEC = _at


class Count:

    def __init__(self, sem):
        self.sem, self.n, self.turn = sem, 0, 0

    def inc(self, ins):
        self.n += 1
        return ins.then_inc(self.sem, 1)

    def settle(self, eng, ins):
        self.inc(ins)
        eng.wait_ge(self.sem, self.turn + self.n)


def build(nc, inp, out):
    ctx = ExitStack()
    with ctx:
        def sb(name, shape, dt=F32, st=ctx):
            return st.enter_context(nc.sbuf_tensor(name, shape, dt))

        def sem(name):
            return ctx.enter_context(nc.semaphore(name))

        X = sb("X", [P, KD, T])
        NH = sb("NH", [P, KD, T + TC], F32R)
        NL = sb("NL", [P, KD, T + TC], F32R)
        RAW = [sb(f"RAW{s}", [P, SLOT]) for s in range(2)]
        WH = [sb(f"WH{s}", [P, SLOT], F32R) for s in range(2)]
        WL = [sb(f"WL{s}", [P, SLOT], F32R) for s in range(2)]
        ident, ones = sb("ident", [P, P]), sb("ones", [P, P])
        vecs = sb("vecs", [P, NVEC])
        eps, warm = sb("eps", [P, 1]), sb("warm", [P, 1])
        SA = sb("SA", [P, 2, T + TC])
        VA = sb("VA", [P, 2, T + TC])
        RB = sb("RB", [P, T])
        CV2 = sb("CV2", [P, KD, 2])
        MOD = sb("MOD", [P, NMOD * KD, 2])
        NM, DEN = sb("NM", [P, 4]), sb("DEN", [P, 4])
        GS = sb("GS", [P, 5, KD])
        HG = sb("HG", [P, 3, KD])
        ff = ExitStack()
        HH = sb("HH", [P, HMAX, T + TC], F32R, ff)
        HL = sb("HL", [P, HMAX, T + TC], F32R, ff)
        CX = sb("CX", [P, KD, TC], F32, ff)
        MW = [sb(f"MW{s}", [P, KD, P], F32, ff) for s in range(2)]
        CXIN = sb("CXIN", [P, KD, TC], F32, ff)
        ff.close()
        ld = ExitStack()
        XIN = sb("XIN", [P, T // P, D], F32, ld)
        ld.close()

        a1 = ExitStack()
        QA = sb("QA", [P, 4, T], F32, a1)
        KA = sb("KA", [P, T], F32, a1)
        KPE = sb("KPE", [P, T], F32, a1)
        VAP = sb("VAP", [P, NT, 2, P], F32, a1)
        BIAS = sb("BIAS", [P, NT - 1, T], F32, a1)
        CM = sb("CM", [P, T], F32, a1)
        TB = sb("TB", [P, 2, T], F32, a1)
        PERM = sb("PERM", [P, 4, P], F32, a1)
        M8 = sb("M8", [P, 8], F32, a1)
        early = ExitStack()
        QI = sb("QI", [P, 8, T], F32, early)
        KI = sb("KI", [P, T], F32, early)
        CQ = sb("CQ", [P, 5, T], F32, early)
        TA = sb("TA", [P, 2, T], F32, early)
        WI = sb("WI", [P, NT, IDX_HEADS], F32, early)
        early.close()
        VB = sb("VB", [P, NT, HB, P], F32, a1)
        QB, KB = sb("QB", [P, 4, T], F32, a1), sb("KB", [P, 4, T], F32, a1)
        PT = sb("PT", [P, NT * 8 * P], F32, a1)
        a1.close()

        a2 = ExitStack()
        M = sb("M", [P, KD, T], F32, a2)
        GA = sb("GA", [P, KD, T], F32, a2)
        conv = ExitStack()
        YH, YL = sb("YH", [P, KD, T], F32R, conv), sb("YL", [P, KD, T], F32R, conv)
        conv.close()
        mix = ExitStack()
        MH, ML = sb("MH", [P, KD, T], F32R, mix), sb("ML", [P, KD, T], F32R, mix)
        mix.close()
        QT = sb("QT", [P, HC, T], F32, a2)
        KT = sb("KT", [P, KVC, TK], F32, a2)
        V2 = sb("V2", [P, TK // P, KVC * P], F32, a2)
        PT2 = sb("PT2", [P, TK // P, 4, P], F32, a2)
        TX = sb("TX", [P, 2, T], F32, a2)
        PX = sb("PX", [P, P], F32, a2)
        a2.close()

        PS = ctx.enter_context(nc.psum_tensor("PS", [P, 8 * 512], F32))
        B = [PS[:, i * 512:(i + 1) * 512] for i in range(8)]
        G, U, CG, CU = (B[0], B[2]), (B[1], B[3]), (B[4], B[6]), (B[5], B[7])

        w_loaded = [sem(f"w_loaded{s}") for s in range(2)]
        w_hi, w_lo = sem("w_hi"), sem("w_lo")
        pe_done = sem("pe_done")
        psum_free = sem("psum_free")
        h_split = sem("h_split")
        gate_done = sem("gate_done")
        norm_sq, norm_mm, norm_rms = sem("norm_sq"), sem("norm_mm"), sem("norm_rms")
        norm_x, norm_hi, norm_lo, norm_acc = sem("norm_x"), sem("norm_hi"), sem("norm_lo"), sem("norm_acc")
        mod_loaded = [sem(f"mod_loaded{s}") for s in range(2)]
        mod_s = sem("mod_s")
        mod_done, mod_out = sem("mod_done"), sem("mod_out")
        x_loaded = [sem(f"x_loaded{t}") for t in range(NT)]
        c_loaded, v_loaded = sem("c_loaded"), sem("v_loaded")
        tp_done, tp_out = sem("tp_done"), sem("tp_out")
        rope_y, rope_mm, rope_out = sem("rope_y"), sem("rope_mm"), sem("rope_out")
        lat_out = sem("lat_out")
        a_loaded = sem("a_loaded")
        ix_mm, ix_relu, ix_acc = sem("ix_mm"), sem("ix_relu"), sem("ix_acc")
        v_zero, v_mm, v_out = sem("v_zero"), sem("v_mm"), sem("v_out")
        pj_mm, pj_k, pj_y, pj_sw, pj_out = (sem(f"pj_{c}") for c in ("mm", "k", "y", "sw", "out"))
        at_s, at_m, at_e, at_r, at_t, at_c = (sem(f"at_{c}") for c in "smertc")
        at_v, at_h, at_o, at_d = sem("at_v"), sem("at_h"), sem("at_o"), sem("at_d")
        conv_s = sem("conv_s")
        y_split, y_part = sem("y_split"), sem("y_part")
        ga_done = sem("ga_done")
        hn_sq, hn_mm, hn_rms, hn_z, hn_sw, hn_out = (sem(f"hn_{c}") for c in ("sq", "mm", "rms", "z", "sw", "out"))
        b_loaded = sem("b_loaded")
        v2_mm, v2_out = sem("v2_mm"), sem("v2_out")
        at2_s, at2_m, at2_e, at2_r, at2_t, at2_c = (sem(f"at2_{c}") for c in "smertc")
        at2_v, at2_h, at2_o = sem("at2_v"), sem("at2_h"), sem("at2_o")
        mix_s = sem("mix_s")
        ctx_loaded, ctx_tp, ctx_out = sem("ctx_loaded"), sem("ctx_tp"), sem("ctx_out")
        act_s, dve_s, pool_s, c2_s = sem("act_s"), sem("dve_s"), sem("pool_s"), sem("c2_s")
        out_s = sem("out_s")

        def vec(name, k=0):
            return vecs[:, VEC[name][0] + k:VEC[name][0] + k + 1]

        dmas = []

        def plan(n, d=2):
            dmas.extend([d] * n)
            return len(dmas) - n

        def plan_ffn():
            return [(plan(c), plan(KD // 2)) for c in CHUNKS]

        def loaded(b0, u, i=0):
            return i * 32 + 16 * sum(dmas[(b0 + u) % 2:b0 + u + 1:2])

        ffn1 = plan_ffn()
        w_in_b = [plan(1, 4 if j == 4 else 1 if j == 9 else 2) for j in range(10)][0]
        v_b, pj_b = plan(1), plan(2, 3)
        wo_b = plan(KD // 2)
        ffn2 = plan_ffn()
        ffn3 = plan_ffn()
        conv_b, bg_b, gc_b, ga_b = plan(KD), plan(KD // 2), plan(KD), plan(KD // 2)
        q_b, k_b, v2_b = plan(HC // 2), plan(1), plan(1)
        ba_b, wo2_b = plan(KD // 2), plan(KD // 2)
        ffn4 = plan_ffn()
        NB = len(dmas)
        NF = DFF // P
        G0 = {"ffn1": 0, "ffn2": NF, "ffn3": 2 * NF, "conv": 3 * NF, "gc": 3 * NF + KD, "ffn4": 3 * NF + 2 * KD}
        H0 = {"ffn1": 0, "ffn2": NF, "ffn3": 2 * NF, "ffn4": 3 * NF}
        M0 = {"ffn1": 0, "wo": NF + 12, "ffn2": NF + 12 + KD // 2}
        assert M0["ffn2"] + NF + 12 == NMOD * KD
        WARM = 24
        NCTX = 5 * KD
        MACC = RB[:, :].rearrange("p (t v c) -> p t v c", t=2, v=2)

        def vectors(m0):
            return 2 if m0 < NCTX else 1

        def mod(i, k, v):
            return MOD[:, ds(k + i * KD, 1), v:v + 1].rearrange("p a b -> p (a b)")

        MODULATED = (("norm1", 1, 0), ("norm1", 1, 1), ("norm2", 4, 0), ("norm2", 4, 1), ("norm3", 7, 0))
        HALVED = ((2, 0), (2, 1), (8, 0))
        block = ctx.enter_context(nc.Block())

        def stage(eng, b0, n, straight=False):
            lead = n if straight else 2 if b0 == 0 else 0
            for j in range(lead):
                yield b0 + j, j, (b0 + j) % 2, (loaded(b0, j + 1) if b0 + j + 1 < len(dmas) else None)
            if lead < n:
                with eng.Fori(0, (n - lead) // 2) as i:
                    for u in range(lead, lead + 2):
                        yield i * 2 + (b0 + u), i * 2 + u, (b0 + u) % 2, i * 32 + loaded(b0, u + 1)

        def after(b, n):
            return None if isinstance(b, int) and b + n < 1 else b + n

        def wait(eng, s, value):
            if value is not None:
                eng.wait_ge(s, value)

        norms = []

        class Norm:
            def __init__(self, src, n, tok, gain, dst=None, shift=None, ready=None, early=False):
                self.src, self.n, self.tok, self.gain, self.dst, self.shift = src, n, tok, gain, dst, shift
                self.ready = ready
                self.base, self.no = sum(m.n for m in norms), len(norms)
                self.early, self.sums = early, 3 if early else n
                self.mm, self.acc = sum(m.sums for m in norms), sum(m.n - 3 for m in norms if m.early)
                self.low = sum(m.n for m in norms if m.dst)
                norms.append(self)

        def roots(m):
            return RB[:, 0:T] if m.tok == T else SA[:, 0, T:T + TC]

        def squares(m, k):
            return VA[:, 0, 0:m.tok] if m.early and k == 0 else SA[:, k % 2, 0:m.tok]

        def x_src(k):
            return X[:, k, :]

        def n_dst(k):
            return NH[:, k, 0:T], NL[:, k, 0:T]

        def items_of(n):
            found = []
            for half, t in enumerate(W_IN_TILES[2 * n:2 * n + 2]):
                name, j = t[0], t[1]
                found += {"qi": [("rope", half, QI[:, j, :])] if name == "qi" else None,
                          "qa": [("rope", half, QA[:, j, :])] if name == "qa" else None,
                          "misc": [("twice", half, KI[:, :]), ("kr", half, None), ("wi", half, None)],
                          "kv": [("twice", half, KA[:, :]), ("va", half, None)], "lat": []}[name]
            return found

        ITEMS = [items_of(n) for n in range(10)]
        ITEM0 = [sum(len(x) for x in ITEMS[:n]) for n in range(11)]
        COPIED = [[h for h, t in enumerate(W_IN_TILES[2 * n:2 * n + 2]) if t[0] != "lat"] for n in range(10)]
        COPY0 = [sum(len(x) for x in COPIED[:n]) for n in range(11)]

        UNITS = [("b", h, q) for h in range(HB) for q in range(NT)] + [("a", h, q) for q in range(NT) for h in range(HA)]
        PER_GROUP = 8
        NG = len(UNITS) // PER_GROUP

        def q_scores(u):
            kind, h, q = UNITS[u]
            keys = (q + 1) * P
            if kind == "b":
                return QB[0:96, h % 4, q * P:(q + 1) * P], KB[0:96, h % 4, 0:keys], keys
            r = slice((h % 2) * 64, (h % 2) * 64 + 64)
            return QA[r, h // 2, q * P:(q + 1) * P], KA[r, 0:keys], keys

        def pt_of(u):
            kind, h, q = UNITS[u]
            if kind == "b":
                return PT[:, :].rearrange("p (h s q) -> p h s q", h=2, s=NT)[:, h % 2, 0:q + 1, q * P:(q + 1) * P]
            return PT[:, :].rearrange("p (s h q) -> p s h q", s=NT, h=8)[:, 0:q + 1, (h % 2) * 4 + h // 2, :]

        def heads_out(g, n):
            if g < 4:
                return n[:, 4 + g, 0:T]
            return n[:, 0:4, (g - 4) * P:(g - 3) * P]

        AHEAD = 3
        VF, SF = VA[:, :, :].rearrange("p a t -> p (a t)"), SA[:, :, :].rearrange("p a t -> p (a t)")

        def p_slot(u):
            return (VF[:, (u % 4) * T:(u % 4 + 1) * T] if u % 4 < 3 else SF[:, 2 * T:3 * T])

        def p_slot2(u):
            return (VA, SA)[u % 4 // 2][:, u % 2, :]

        def stat(t, u):
            return t[:, u % 4:u % 4 + 1]

        norm1 = Norm(x_src, KD, T, lambda k: vec("g_ffn1", k), n_dst, ready=lambda k: (tp_out, 25 + k))

        def pj_bank(i):
            return B[(6, 5)[i % 2]][0:96, :]

        def stream_ready(stages):
            return lambda k: (psum_free, stages[-1][1] + k // 2 + 1)

        norm_mix = Norm(x_src, KD, T, lambda k: vec("g_mix", k), n_dst, ready=stream_ready(ffn1), early=True)
        norm_q = Norm(lambda k: CQ[:, k, :], 3, T, lambda k: vec("g_q_lat", k), n_dst,
                      ready=lambda k: (lat_out, k + 1))
        norm_kv = Norm(lambda k: CQ[:, 3 + k, :], 2, T, lambda k: vec("g_kv_lat", k), lambda k: n_dst((3, 7)[k]),
                       ready=lambda k: (lat_out, k + 4))
        norm2 = Norm(x_src, KD, T, lambda k: vec("g_ffn2", k), n_dst,
                     ready=lambda k: (psum_free, wo_b + k // 2 + 1), early=True)
        norm_final = Norm(x_src, KD, T, lambda k: vec("g_final", k), None, ready=stream_ready(ffn2), early=True)

        def c_src(k):
            return CX[:, k, :]

        def ctx_in(t):
            return CXIN[:, t * 4:t * 4 + 4, :]

        def c_dst(k):
            return NH[:, k, T:T + TC], NL[:, k, T:T + TC]

        def modulated(which, src, tok, dst, ready, early=False):
            i, v = MODULATED[which][1] - 1, MODULATED[which][2]
            return Norm(src, KD, tok, lambda k: GS[:, which, k:k + 1], dst,
                        shift=lambda k: MOD[:, i * KD + k, v:v + 1], ready=ready, early=early)

        norm_c1 = modulated(1, c_src, TC, c_dst, lambda k: (ctx_out, 2 * TC // P))
        norm_x1 = modulated(0, x_src, T, n_dst, lambda k: (norm_x, norm_final.base + k + 1))
        norm_x2 = modulated(2, x_src, T, n_dst, stream_ready(ffn3), True)
        norm_c2 = modulated(3, c_src, TC, c_dst, stream_ready(ffn3))
        norm_x3 = modulated(4, x_src, T, n_dst, lambda k: (psum_free, wo2_b + k // 2 + 1), True)
        norm_out = Norm(x_src, KD, T, lambda k: vec("final", k), None, ready=stream_ready(ffn4), early=True)

        HN = [(q_b + j // 2, 0, j % 2, T, "q_norm", QT[:, j, :]) for j in range(HC)]
        HN += [(k_b, 0, j, T, "k_norm", KT[:, j, TC:TK]) for j in range(KVC)]
        HN += [(k_b, 1, j, TC, "k_norm", KT[:, j, 0:TC]) for j in range(KVC)]

        def hn_of(b):
            return [i for i, h in enumerate(HN) if h[0] == b]

        def hn_waves(b):
            return [hn_of(b)[w:w + 2] for w in range(0, len(hn_of(b)), 2)]

        def hn_bank(i):
            b, other, half, tok = HN[i][:4]
            return (G, U)[half][(b + other) % 2][:, 0:tok]

        UNITS2 = [(g, q, e) for g in range(KVC) for q in range(NT) for e in range(4)]

        @block.sync
        def _(sp):
            sp.dma_start(ident[:, :], inp["ident"]).then_inc(c_loaded, 16)
            for t in range(NT):
                sp.dma_start(XIN[:, t, :], inp["x"][0][t * P:(t + 1) * P, :]).then_inc(x_loaded[t], 16)
            sp.dma_start(vecs[:, :], inp["vecs"]).then_inc(v_loaded, 16)

            def weights(w, k0, kn, c0, n):
                return w[k0 * P:(k0 + kn) * P, :].rearrange("(k p) n -> p k n", p=P)[:, :, ds(c0, n)]

            def mods(b0, j, s, m0):
                if m0 is None:
                    return
                t = (s + b0) % 2
                if m0 == M0["wo"]:
                    sp.wait_ge(at_o, NG)
                if not (isinstance(j, int) and j + m0 < 2):
                    sp.wait_ge(mod_s, j * KD + KD * (m0 - 1))
                sp.dma_start(MW[t][:, :, :], weights(inp["w_mod_2"][0], 0, KD, j * P + m0 * P, P))\
                    .then_inc(mod_loaded[t], 16)

            def gate_up(b0, n, wg, cg, wu, cu, m0=None):
                for b, j, s, _ in stage(sp, b0, n):
                    wait(sp, w_lo, after(b, -1))
                    raw = RAW[s][:, :].rearrange("p (h k c) -> p h k c", h=2, k=KD)
                    sp.dma_start(raw[:, 0], weights(wg, 0, KD, j * P + cg, P)).then_inc(w_loaded[s], 16)
                    sp.dma_start(raw[:, 1], weights(wu, 0, KD, j * P + cu, P)).then_inc(w_loaded[s], 16)
                    mods(b0, j, s, m0)

            def pairs(b0, n, w, k0, kn, c0, straight=False, m0=None):
                for b, j, s, _ in stage(sp, b0, n, straight):
                    wait(sp, w_lo, after(b, -1))
                    raw = RAW[s][:, 0:kn * 2 * P].rearrange("p (k c) -> p k c", k=kn)
                    h = kn // 2
                    sp.dma_start(raw[:, 0:h], weights(w, k0, h, j * (2 * P) + c0, 2 * P)).then_inc(w_loaded[s], 16)
                    sp.dma_start(raw[:, h:kn], weights(w, k0 + h, kn - h, j * (2 * P) + c0, 2 * P))\
                        .then_inc(w_loaded[s], 16)
                    mods(b0, j, s, m0)

            def ffn(stages, wg, cg, wu, cu, wd, last=False, m0=None):
                k0 = 0
                for c, (kn, (bg, bd)) in enumerate(zip(CHUNKS, stages)):
                    gate_up(bg, kn, wg, cg + k0 * P, wu, cu + k0 * P, m0)
                    m1 = None if m0 is None else m0 + kn
                    pairs(bd, KD // 2, wd, k0, kn, 0, last and c == 2, m1)
                    m0 = None if m0 is None else m1 + KD // 2
                    k0 += kn

            ffn(ffn1, inp["w1_gate"][0], 0, inp["w1_up"][0], 0, inp["w1_down"][0], m0=M0["ffn1"])
            w_in, w_uq, w_ukv = inp["w_in"][0], inp["w_uq"][0], inp["w_ukv"][0]
            for n in range(10):
                b = w_in_b + n
                s = b % 2
                sp.wait_ge(w_lo, b - 1)
                raw = RAW[s][:, :].rearrange("p (h k c) -> p h k c", h=2, k=KD)
                for half, (name, j, c) in enumerate(W_IN_TILES[2 * n:2 * n + 2]):
                    for c0, width, at in (MISC if name == "misc" else ((c, P, 0),)):
                        sp.dma_start(raw[:, half, :, at:at + width],
                                     w_in[:, c0:c0 + width].rearrange("(k p) n -> p k n", p=P)).then_inc(w_loaded[s], 16)
                if n == 0:
                    sp.wait_ge(pe_done, w_in_b)
                    sp.wait_ge(mod_s, KD * M0["wo"])
                    for dst, src in ((TA, "rope64"), (TB, "rope96"), (PERM, "perms")):
                        sp.dma_start(dst[:, :, :], inp[src]).then_inc(a_loaded, 16)
                    sp.dma_start(CM[:, :], inp["causal"]).then_inc(a_loaded, 16)
            s = v_b % 2
            sp.wait_ge(w_lo, v_b - 1)
            for k in range(2):
                sp.dma_start(RAW[s][:, k * 512:(k + 1) * 512].rearrange("p (h c) -> p h c", h=HB),
                             w_ukv[k * P:(k + 1) * P].rearrange("p (h c) -> p h c", h=HB)[:, :, 64:128])\
                    .then_inc(w_loaded[s], 16)
            for n in range(2):
                b = pj_b + n
                s = b % 2
                sp.wait_ge(w_lo, b - 1)
                sp.dma_start(RAW[s][:, 0:1152].rearrange("p (k c) -> p k c", k=3),
                             w_uq[:, n * 384:(n + 1) * 384].rearrange("(k p) n -> p k n", p=P)).then_inc(w_loaded[s], 16)
                for k in range(2):
                    sp.dma_start(RAW[s][:, 1152 + k * 256:1408 + k * 256].rearrange("p (h c) -> p h c", h=4),
                                 w_ukv[k * P:(k + 1) * P].rearrange("p (h c) -> p h c", h=HB)[:, 4 * n:4 * n + 4, 0:64])\
                        .then_inc(w_loaded[s], 16)
            pairs(wo_b, KD // 2, inp["w_out"][0], 0, KD, 0, m0=M0["wo"])
            for t in range(TC // P):
                sp.dma_start(ctx_in(t), inp["ctx_2"][0][t * P:(t + 1) * P, :].rearrange("p (k c) -> p k c", c=TC))\
                    .then_inc(ctx_loaded, 16)
            ffn(ffn2, inp["w2_gate"][0], 0, inp["w2_up"][0], 0, inp["w2_down"][0], m0=M0["ffn2"])
            w1, w2, w_in2 = inp["ffn1_w_in_2"][0], inp["ffn2_w_in_2"][0], inp["w_in_2"][0]
            ffn(ffn3, w1, 0, w1, DFF, inp["ffn1_w_out_2"][0])
            gate_up(conv_b, KD, w_in2, D, w_in2, 2 * D)
            pairs(bg_b, KD // 2, w_in2, 0, KD, 0)
            gate_up(gc_b, KD, w_in2, 4608, inp["w_branch_conv_2"][0], 0)
            pairs(ga_b, KD // 2, w_in2, 0, KD, 4608 + D)
            sp.wait_ge(pe_done, ga_b)
            sp.dma_start(TX[:, :, :], inp["rope128"]).then_inc(b_loaded, 16)
            sp.dma_start(PX[:, :], inp["perms"][:, 0, :]).then_inc(b_loaded, 16)
            pairs(q_b, HC // 2, w_in2, 0, KD, 3072)
            pairs(k_b, 1, w_in2, 0, KD, 4096, True)
            pairs(v2_b, 1, w_in2, 0, KD, 4352, True)
            pairs(ba_b, KD // 2, inp["w_branch_attn_2"][0], 0, KD, 0)
            pairs(wo2_b, KD // 2, inp["w_out_2"][0], 0, KD, 0)
            ffn(ffn4, w2, 0, w2, DFF, inp["ffn2_w_out_2"][0], True)
            for t in range(NT):
                sp.wait_ge(tp_out, 32 + KD * (t + 1))
                sp.dma_start(out[0][t * P:(t + 1) * P, :], XIN[:, t, :]).then_inc(out_s, 16)
            sp.wait_ge(out_s, 16 * NT)

        @block.tensor
        def _(pe):
            def transposes(src_of, no, first_waits):
                for t in range(32):
                    if first_waits and t % KD == 0:
                        pe.wait_ge(first_waits[t // KD], 16)
                    if t >= 4:
                        pe.wait_ge(tp_out, no * 32 + t - 3)
                    pe.transpose(B[t % 4][:, 0:P], src_of(t), ident[:, :]).then_inc(tp_done, 1)

            def norm(m, banks_free):
                if m is norm_x2:
                    pe.wait_ge(psum_free, banks_free)
                for k in ((0, m.n - 2, m.n - 1) if m.early else range(m.n)):
                    if m.early and k == 0:
                        pe.wait_ge(norm_acc, m.acc + m.n - 3)
                    else:
                        pe.wait_ge(norm_sq, m.base + k + 1)
                    pe.matmul(B[7][:, 0:m.tok], ones[:, :], squares(m, k),
                              start=k == 0, stop=k == m.n - 1).then_inc(norm_mm, 1)
                wait(pe, psum_free, banks_free)
                if m.dst and m.tok == T and m.n == KD:
                    busy(WARM)

            def busy(n):
                for _ in range(n):
                    pe.matmul(B[6][:, 0:P], ident[:, :], ones[:, :], start=True, stop=True)

            def begin(b):
                pe.wait_ge(w_lo, b + 1)
                wait(pe, psum_free, after(b, -1))

            def tile(outs, wt, xs, kn, ready=None):
                for k in range(kn):
                    if ready is not None:
                        pe.wait_ge(ready[0], ready[1] + k + 1)
                    wh, wl = wt(k)
                    for o, (xh, xl) in zip(outs, xs):
                        pe.matmul(o, wh, xh(k), start=k == 0, stop=False)
                        pe.matmul(o, wh, xl(k), start=False, stop=False)
                    for o, (xh, xl) in zip(outs, xs):
                        last = pe.matmul(o, wl, xh(k), start=False, stop=k == kn - 1)
                return last

            def tiles(outs, wt, xs, kn, ready=None):
                for k in range(kn):
                    if ready is not None:
                        pe.wait_ge(ready[0], ready[1] + k + 1)
                    for half in range(2):
                        wh, wl = wt(half, k)
                        for o, (xh, xl) in zip(outs[half], xs):
                            pe.matmul(o, wh, xh(k), start=k == 0, stop=False)
                            pe.matmul(o, wh, xl(k), start=False, stop=False)
                        for o, (xh, xl) in zip(outs[half], xs):
                            last = pe.matmul(o, wl, xh(k), start=False, stop=k == kn - 1)
                return last

            def part(h, l, a, b):
                return (lambda k: h[:, k, a:b]), (lambda k: l[:, k, a:b])

            def mods(b0, j, s, m0):
                if m0 is None:
                    return
                t = (s + b0) % 2
                pe.wait_ge(mod_s, j * KD + KD * (m0 + 1))
                wait(pe, mod_out, after(j + m0, -1))
                for v in range(vectors(m0)):
                    last = pe.matmul(B[4 + t][:, v:v + 1], MACC[:, t, v, :], ones[:, 0:1], start=True, stop=True)
                last.then_inc(mod_done, 1)

            def gate_up(b0, n, xs, banks, ready, m0=None, xu=None, ready_u=None):
                for b, j, s, _ in stage(pe, b0, n):
                    begin(b)

                    def wt(half, k):
                        c = (half * KD + k) * P
                        return WH[s][:, c:c + P], WL[s][:, c:c + P]
                    if xu:
                        tile(banks[0][s], lambda k: wt(0, k), xs, KD, ready)
                        last = tile(banks[1][s], lambda k: wt(1, k), xu, KD, ready_u)
                    else:
                        last = tiles((banks[0][s], banks[1][s]), wt, xs, KD, ready)
                    last.then_inc(pe_done, 1)
                    mods(b0, j, s, m0)

            def pairs(b0, n, xs, banks, kn, ready=None, straight=False, m0=None):
                for b, j, s, _ in stage(pe, b0, n, straight):
                    begin(b)

                    def wt(half, k):
                        c = (k * 2 + half) * P
                        return WH[s][:, c:c + P], WL[s][:, c:c + P]
                    last = tiles((banks[0][s], banks[1][s]), wt, xs, kn, ready)
                    last.then_inc(pe_done, 1)
                    mods(b0, j, s, m0)

            xb = [[[G[s][:, :]] for s in range(2)], [[U[s][:, :]] for s in range(2)]]
            xcb = [[[G[s][:, :], CG[s][:, 0:TC]] for s in range(2)], [[U[s][:, :], CU[s][:, 0:TC]] for s in range(2)]]
            XS = [part(NH, NL, 0, T)]
            XCS = XS + [part(NH, NL, T, T + TC)]
            HS = [part(HH, HL, 0, T)]
            HCS = HS + [part(HH, HL, T, T + TC)]

            def ffn(stages, m, h0, xs, hs, banks, last=False, m0=None):
                for c, (kn, (bg, bd)) in enumerate(zip(CHUNKS, stages)):
                    gate_up(bg, kn, xs, banks, (norm_lo, m.low) if c == 0 else None, m0)
                    m1 = None if m0 is None else m0 + kn
                    pairs(bd, KD // 2, hs, banks, kn, (h_split, h0), last and c == 2, m1)
                    m0 = None if m0 is None else m1 + KD // 2
                    h0 += kn

            pe.wait_ge(c_loaded, 16)
            pe.wait_ge(c2_s, 2)
            transposes(lambda t: XIN[:, t // KD, (t % KD) * P:(t % KD + 1) * P], 0, x_loaded)
            norm(norm1, None)
            ffn(ffn1, norm1, H0["ffn1"], XS, HS, xb, m0=M0["ffn1"])
            norm(norm_mix, w_in_b)

            def items(n):
                for i, (kind, half, _) in enumerate(ITEMS[n], ITEM0[n]):
                    y = COPY0[n] + COPIED[n].index(half)
                    src = SA[:, y % 2, 0:T]
                    pe.wait_ge(rope_y, y + 1)
                    if i >= 2:
                        pe.wait_ge(rope_out, i - 1)
                    o = B[4 + i % 2]
                    if kind in ("wi", "va"):
                        for t in range(NT):
                            last = pe.transpose(o[:, t * P:(t + 1) * P], src[:, t * P:(t + 1) * P], ident[:, :])
                    else:
                        if kind == "twice":
                            pe.matmul(B[6 + i % 2][:, :], PERM[:, 1, :], src, start=True, stop=True)
                        p = {"rope": 0, "twice": 2, "kr": 3}[kind]
                        last = pe.matmul(o[:, :], PERM[:, p, :], src, start=True, stop=True)
                    last.then_inc(rope_mm, 1)

            for n in range(10):
                b = w_in_b + n
                s = b % 2
                begin(b)

                def wt(half, k):
                    c = (half * KD + k) * P
                    return WH[s][:, c:c + P], WL[s][:, c:c + P]
                if n == 0:
                    last = tiles(((G[s][:, :],), (U[s][:, :],)), wt, XS, KD, (norm_lo, norm_mix.low))
                for half in range(len(W_IN_TILES[2 * n:2 * n + 2])) if n else ():
                    last = tile(((G, U)[half][s][:, :],), lambda k: wt(half, k), XS, KD)
                    if half == 0:
                        if n == 1:
                            pe.wait_ge(a_loaded, 64)
                        if len(W_IN_TILES[2 * n:2 * n + 2]) == 2:
                            items(n - 1)
                last.then_inc(pe_done, 1)
            pe.wait_ge(rope_out, ITEM0[10])
            norm(norm_q, v_b)
            norm(norm_kv, None)

            n = 0
            for q in range(1, NT):
                for h in range(IDX_HEADS):
                    if n >= 2:
                        pe.wait_ge(ix_relu, n - 1)
                    r = slice((h % 2) * 64, (h % 2) * 64 + 64)
                    pe.matmul(B[n % 2][:, 0:(q + 1) * P], QI[r, h // 2, q * P:(q + 1) * P], KI[r, 0:(q + 1) * P],
                              start=True, stop=True).then_inc(ix_mm, 1)
                    n += 1

            begin(v_b)
            s = v_b % 2
            for t in range(NT):
                if t >= 2:
                    pe.wait_ge(v_out, t - 1)
                if t == 0:
                    pe.wait_ge(norm_lo, norm_kv.low + 2)
                for k in range(2):
                    xh, xl = (z[:, (3, 7)[k], t * P:(t + 1) * P] for z in (NH, NL))
                    wh, wl = (z[s][:, k * 512:(k + 1) * 512] for z in (WH, WL))
                    pe.matmul(B[2 + t % 2][:, :], xh, wh, start=k == 0, stop=False)
                    pe.matmul(B[2 + t % 2][:, :], xh, wl, start=False, stop=False)
                    last = pe.matmul(B[2 + t % 2][:, :], xl, wh, start=False, stop=k == 1)
                last.then_inc(v_mm, 1)
            pe.wait_ge(v_out, NT)
            pe.sem_inc(pe_done, 1)

            def project(n):
                b = pj_b + n
                s = b % 2
                begin(b)
                def q_product(i):
                    if i >= 2:
                        pe.wait_ge(pj_out, 4 * n + i - 1)
                    for k in range(3):
                        xh, xl = (z[:, k, 0:T] for z in (NH, NL))
                        wh, wl = (z[s][:, k * 384 + i * 96:k * 384 + i * 96 + 96] for z in (WH, WL))
                        pe.matmul(pj_bank(i), wh, xh, start=k == 0, stop=False)
                        pe.matmul(pj_bank(i), wh, xl, start=False, stop=False)
                        pe.matmul(pj_bank(i), wl, xh, start=False, stop=k == 2)

                q_product(0)
                for i in range(4):
                    if i or n:
                        pe.wait_ge(pj_k, 4 * n + i)
                    for k in range(2):
                        xh, xl = (z[:, (3, 7)[k], 0:T] for z in (NH, NL))
                        c = 1152 + k * 256 + i * 64
                        wh, wl = (z[s][:, c:c + 64] for z in (WH, WL))
                        pe.matmul(B[7][0:64, :], wh, xh, start=k == 0, stop=False)
                        pe.matmul(B[7][0:64, :], wh, xl, start=False, stop=False)
                        last = pe.matmul(B[7][0:64, :], wl, xh, start=False, stop=k == 1)
                    last.then_inc(pj_mm, 1)
                    if i < 3:
                        q_product(i + 1)
                    pe.wait_ge(pj_y, 4 * n + i + 1)
                    if n and i == 0:
                        pe.wait_ge(at_o, 1)
                    if i or n:
                        pe.wait_ge(pj_out, 4 * n + i)
                    pe.matmul(B[4][0:96, :], PERM[0:96, 3, 0:96], SF[0:96, (i % 2) * T:(i % 2 + 1) * T],
                              start=True, stop=True).then_inc(pj_sw, 1)
                pe.wait_ge(pj_sw, 4 * n + 4)
                pe.sem_inc(pe_done, 1)

            def scores(u):
                if u >= 2:
                    pe.wait_ge(at_m, u - 1)
                q, k, keys = q_scores(u)
                pe.matmul(B[u % 2][:, 0:keys], q, k, start=True, stop=True).then_inc(at_s, 1)

            def turn(u):
                pe.wait_ge(at_r, u + 1)
                if u >= 2:
                    pe.wait_ge(at_c, u - 1)
                for t in range(UNITS[u][2] + 1):
                    last = pe.transpose(B[2 + u % 2][:, t * P:(t + 1) * P], p_slot(u)[:, t * P:(t + 1) * P], ident[:, :])
                last.then_inc(at_t, 1)

            def heads(g):
                pe.wait_ge(at_c, PER_GROUP * (g + 1))
                if g:
                    pe.wait_ge(at_o, g)
                if g < 2:
                    pe.wait_ge(pj_out, 4 * g + 4)
                first = True
                if g < 4:
                    for h in range(2):
                        for t in range(NT):
                            last = pe.matmul(B[4][:, t * P:T], VB[:, t, 2 * g + h, :],
                                             PT[:, :].rearrange("p (h s q) -> p h s q", h=2, s=NT)[:, h, t, t * P:T],
                                             start=first, stop=h == 1 and t == NT - 1)
                            first = False
                else:
                    for t in range(g - 3):
                        for h in range(2):
                            last = pe.matmul(B[4][:, :], VAP[:, t, h, :], PT[:, (t * 8 + h * 4) * P:(t * 8 + h * 4 + 4) * P],
                                             start=first, stop=h == 1 and t == g - 4)
                            first = False
                last.then_inc(at_v, 1)

            for u in range(-AHEAD, len(UNITS)):
                if u + AHEAD in (0, 16):
                    project((u + AHEAD) // 16)
                if u + AHEAD < len(UNITS):
                    scores(u + AHEAD)
                if u >= 0:
                    turn(u)
                    if u % PER_GROUP == PER_GROUP - 1:
                        heads(u // PER_GROUP)

            pe.wait_ge(at_o, NG)
            pairs(wo_b, KD // 2, XS, xb, KD, m0=M0["wo"])
            norm(norm2, ffn2[0][0])
            ffn(ffn2, norm2, H0["ffn2"], XS, HS, xb, m0=M0["ffn2"])
            norm(norm_final, ffn3[0][0])

            pe.wait_ge(ctx_loaded, 16 * (TC // P))
            for n in range(2 * TC // P):
                for f in range(4):
                    o = (n % 2) * 4 + f
                    last = pe.transpose(B[n][:, f * P:(f + 1) * P], ctx_in(n // 2)[:, o // 2, (o % 2) * P:(o % 2 + 1) * P],
                                        ident[:, :])
                last.then_inc(ctx_tp, 1)
            pe.wait_ge(norm_rms, norm_final.no + 1)
            norm(norm_c1, None)
            pe.wait_ge(norm_rms, norm_c1.no + 1)
            norm(norm_x1, None)
            ffn(ffn3, norm_x1, H0["ffn3"], XCS, HCS, xcb)
            norm(norm_x2, conv_b)
            pe.wait_ge(norm_rms, norm_x2.no + 1)
            norm(norm_c2, None)
            gate_up(conv_b, KD, XS, xb, (norm_lo, norm_x2.low))
            pairs(bg_b, KD // 2, XS, xb, KD)
            gate_up(gc_b, KD, XS, xb, None, xu=[part(YH, YL, 0, T)], ready_u=(y_split, 0))
            pairs(ga_b, KD // 2, XS, xb, KD)

            def head_sums(b):
                for i in hn_of(b):
                    tok = HN[i][3]
                    pe.wait_ge(hn_sq, i + 1)
                    if i >= 2:
                        pe.wait_ge(hn_rms, i - 1)
                    pe.matmul(B[4 + i % 2][:, 0:tok], ones[:, :], SA[:, i % 2, 0:tok], start=True, stop=True)\
                        .then_inc(hn_mm, 1)

            def head_swaps(b):
                for i in hn_of(b):
                    if HN[i][3] == T:
                        pe.wait_ge(hn_z, i + 1)
                        if i >= 2:
                            pe.wait_ge(hn_out, i - 1)
                        pe.matmul(B[6 + i % 2][:, :], PX[:, :], VA[:, i % 2, 0:T], start=True, stop=True)\
                            .then_inc(hn_sw, 1)

            pe.wait_ge(b_loaded, 32)
            for n in range(HC // 2 + 1):
                b = q_b + n
                s = b % 2
                if b == k_b:
                    pe.wait_ge(w_lo, b + 1)
                    head_sums(b - 1)
                    head_swaps(b - 1)
                    pe.wait_ge(psum_free, b)
                else:
                    begin(b)
                for half in range(2):
                    def wt(k):
                        c = (k * 2 + half) * P
                        return WH[s][:, c:c + P], WL[s][:, c:c + P]
                    if b == k_b:
                        last = tile([(G, U)[half][s][:, :], (G, U)[half][1 - s][:, 0:TC]], wt, XCS, KD,
                                    (norm_lo, norm_c2.low))
                    else:
                        last = tile([(G, U)[half][s][:, :]], wt, XS, KD)
                        if n and half == 0:
                            head_sums(b - 1)
                        if n and half == 1:
                            head_swaps(b - 1)
                last.then_inc(pe_done, 1)
            head_sums(k_b)
            head_swaps(k_b)
            pe.wait_ge(psum_free, v2_b)
            pe.wait_ge(hn_out, len(HN))
            pe.wait_ge(w_lo, v2_b + 1)
            s = v2_b % 2
            for t in range(TK // P):
                if t >= 4:
                    pe.wait_ge(v2_out, t - 3)
                c = (T + t * P) % TK
                for k in range(KD):
                    xh, xl = (z[:, k, c:c + P] for z in (NH, NL))
                    wh, wl = (z[s][:, k * 2 * P:(k + 1) * 2 * P] for z in (WH, WL))
                    o = B[t % 4][:, 0:2 * P]
                    pe.matmul(o, xh, wh, start=k == 0, stop=False)
                    pe.matmul(o, xh, wl, start=False, stop=False)
                    last = pe.matmul(o, xl, wh, start=False, stop=k == KD - 1)
                last.then_inc(v2_mm, 1)
            pe.wait_ge(v2_out, TK // P)
            pe.sem_inc(pe_done, 1)

            def scores2(u):
                g, q, e = UNITS2[u]
                if u >= 2:
                    pe.wait_ge(at2_e, u - 1)
                for k0, k1 in ((0, T), (T, TK)):
                    last = pe.matmul(PS[:, (u % 2) * 1024 + k0:(u % 2) * 1024 + k1],
                                     QT[:, g * 4 + e, q * P:(q + 1) * P], KT[:, g, k0:k1], start=True, stop=True)
                last.then_inc(at2_s, 1)

            def turn2(u):
                pe.wait_ge(at2_r, u + 1)
                for x in range(2):
                    n = 2 * u + x
                    if n >= 3:
                        pe.wait_ge(at2_c, n - 2)
                    for t in range(3):
                        last = pe.transpose(B[4 + n % 3][:, t * P:(t + 1) * P],
                                            p_slot2(u)[:, (3 * x + t) * P:(3 * x + t + 1) * P], ident[:, :])
                    last.then_inc(at2_t, 1)

            def heads2(n):
                pe.wait_ge(at2_c, 8 * (n + 1))
                if n:
                    pe.wait_ge(at2_o, n)
                for t in range(TK // P):
                    last = pe.matmul(B[7][:, :], V2[:, t, (n // NT) * P:(n // NT + 1) * P], PT2[:, t, :, :],
                                     start=t == 0, stop=t == TK // P - 1)
                last.then_inc(at2_v, 1)

            for u in range(-AHEAD, len(UNITS2)):
                if u + AHEAD < len(UNITS2):
                    scores2(u + AHEAD)
                if u >= 0:
                    turn2(u)
                    if u % 4 == 3:
                        heads2(u // 4)
            pe.wait_ge(at2_o, KVC * NT)
            pairs(ba_b, KD // 2, XS, xb, KD)
            pairs(wo2_b, KD // 2, [part(MH, ML, 0, T)], xb, KD, (y_split, KD))
            norm(norm_x3, ffn4[0][0])
            ffn(ffn4, norm_x3, H0["ffn4"], XS, HS, xb, True)
            norm(norm_out, NB)
            pe.wait_ge(norm_x, norm_out.base + KD)
            transposes(lambda t: X[:, t % KD, (t // KD) * P:(t // KD + 1) * P], 1, None)

        @block.scalar
        def _(act):
            def split(s, at, b):
                act.wait_ge(w_loaded[1 - s], at)
                wait(act, pe_done, after(b, 0))
                act.activation(WH[1 - s][:, :], RAW[1 - s][:, :], ACT.Copy).then_inc(w_hi, 1)

            def norm_roots(m):
                act.activation(warm[:, :], eps[:, :], ACT.Sqrt)
                for k in range(m.n):
                    act.wait_ge(*m.ready(k))
                    if m.early and k >= 3:
                        act.wait_ge(norm_acc, m.acc + k - 2)
                    if not m.early and k >= 2:
                        act.wait_ge(norm_mm, m.mm + k - 1)
                    act.activation(squares(m, k), m.src(k), ACT.Square).then_inc(norm_sq, 1)
                act.wait_ge(norm_mm, m.mm + m.sums)
                act.activation(roots(m), B[7][:, 0:m.tok], ACT.Sqrt, bias=eps[:, :],
                               scale=1.0 / (m.n * P)).then_inc(norm_rms, 1)

            def norm_high(m):
                if m.dst:
                    for k in range(m.n):
                        act.wait_ge(norm_x, m.base + k + 1)
                        if m.shift:
                            ins = act.activation(m.dst(k)[0], VA[:, k % 2, 0:m.tok], ACT.Identity, bias=m.shift(k))
                        else:
                            ins = act.activation(m.dst(k)[0], VA[:, k % 2, 0:m.tok], ACT.Copy)
                        ins.then_inc(norm_hi, 1)

            def norm(m):
                norm_roots(m)
                norm_high(m)

            def gate_up(b0, n, tok, func=ACT.Silu):
                for b, j, s, at in stage(act, b0, n):
                    split(s, at, b)
                    act.wait_ge(pe_done, b + 1)
                    wait(act, psum_free, after(b, -1))
                    if tok > T:
                        act.activation(SA[:, s, T:tok], CG[s][:, 0:tok - T], func)
                    act.activation(SA[:, s, 0:T], G[s][:, :], func).then_inc(gate_done, 1)

            def only_split(b0, n, straight=False):
                for b, j, s, at in stage(act, b0, n, straight):
                    if at is not None:
                        split(s, at, b)

            def ffn(stages, tok, last=False):
                for c, (kn, (bg, bd)) in enumerate(zip(CHUNKS, stages)):
                    gate_up(bg, kn, tok)
                    only_split(bd, KD // 2, last and c == 2)

            act.wait_ge(w_loaded[0], loaded(0, 0))
            act.activation(WH[0][:, :], RAW[0][:, :], ACT.Copy).then_inc(w_hi, 1)
            act.wait_ge(c2_s, 2)
            act.wait_ge(v_loaded, 16)
            for v, name in enumerate(("c", "c_ctx")):
                last = act.activation(CV2[:, :, v], vecs[:, VEC[name][0]:VEC[name][0] + KD], ACT.Silu)
            last.then_inc(act_s, 1)
            norm(norm1)
            ffn(ffn1, T)
            norm(norm_mix)
            for n in range(10):
                b = w_in_b + n
                split(b % 2, loaded(b, 1), b)
                for i, half in enumerate(COPIED[n], COPY0[n]):
                    if i == COPY0[n]:
                        act.wait_ge(pe_done, b + 1)
                    if i >= 2:
                        done = [ITEM0[m] + len([x for x in ITEMS[m] if x[1] <= h]) for m in range(10) for h in COPIED[m]]
                        act.wait_ge(rope_mm, done[i - 2])
                    act.activation(SA[:, i % 2, 0:T], (G, U)[half][b % 2][:, :], ACT.Copy).then_inc(rope_y, 1)
            norm(norm_q)
            norm(norm_kv)
            n = 0
            for q in range(1, NT):
                for h in range(IDX_HEADS):
                    act.wait_ge(ix_mm, n + 1)
                    if n >= 2:
                        act.wait_ge(ix_acc, n - 1)
                    act.activation(SA[:, n % 2, 0:(q + 1) * P], B[n % 2][:, 0:(q + 1) * P], ACT.Relu).then_inc(ix_relu, 1)
                    n += 1
            split(v_b % 2, loaded(v_b, 1), v_b)

            def project(n):
                b = pj_b + n
                split(b % 2, loaded(b, 1), b)
                for i in range(4):
                    act.wait_ge(pj_mm, 4 * n + i + 1)
                    if 4 * n + i >= 2:
                        act.wait_ge(pj_sw, 4 * n + i - 1)
                    act.activation(SF[0:96, (i % 2) * T:(i % 2 + 1) * T], pj_bank(i), ACT.Copy).then_inc(pj_y, 1)

            def exp(u):
                act.wait_ge(at_m, u + 1)
                keys = (UNITS[u][2] + 1) * P
                p = p_slot(u)[:, 0:keys]
                act.activation(p, p, ACT.Exp, bias=stat(NM, u), accum_out=stat(DEN, u))\
                    .then_inc(at_e, 1)

            def normalised(u):
                keys = (UNITS[u][2] + 1) * P
                act.wait_ge(at_d, u + 1)
                p = p_slot(u)[:, 0:keys]
                act.activation(p, p, ACT.Copy, scale=stat(DEN, u)).then_inc(at_r, 1)

            def turned(u):
                g = u // PER_GROUP
                act.wait_ge(at_t, u + 1)
                if u % PER_GROUP == 0 and g:
                    act.wait_ge(at_v, g)
                keys = (UNITS[u][2] + 1) * P
                act.activation(pt_of(u), B[2 + u % 2][:, 0:keys].rearrange("p (s q) -> p s q", q=P), ACT.Copy)\
                    .then_inc(at_c, 1)

            def heads(g):
                act.wait_ge(at_v, g + 1)
                o = heads_out(g, NH)
                i = B[4][:, :] if g < 4 else B[4][:, :].rearrange("p (h q) -> p h q", h=4)
                act.activation(o, i, ACT.Copy).then_inc(at_h, 1)

            for u in range(-AHEAD, len(UNITS)):
                if u + AHEAD in (0, 16):
                    project((u + AHEAD) // 16)
                if 0 <= u + AHEAD - 1 < len(UNITS):
                    exp(u + AHEAD - 1)
                if 0 <= u + 1 < len(UNITS):
                    normalised(u + 1)
                if u >= 0:
                    if u % PER_GROUP == 0 and u:
                        heads(u // PER_GROUP - 1)
                    turned(u)
            heads(NG - 1)
            only_split(wo_b, KD // 2)
            norm(norm2)
            ffn(ffn2, T)
            norm(norm_final)

            for n in range(2 * TC // P):
                act.wait_ge(ctx_tp, n + 1)
                act.activation(CX[:, (n % 2) * 4:(n % 2) * 4 + 4, (n // 2) * P:(n // 2 + 1) * P],
                               B[n][:, :].rearrange("p (f c) -> p f c", f=4), ACT.Copy).then_inc(ctx_out, 1)
            norm_roots(norm_c1)
            norm_roots(norm_x1)
            norm_high(norm_c1)
            norm_high(norm_x1)
            ffn(ffn3, T + TC)
            norm_roots(norm_x2)
            norm_roots(norm_c2)
            norm_high(norm_x2)
            gate_up(conv_b, KD, T, func=ACT.Copy)
            for b, j, s, at in stage(act, bg_b, KD // 2, True):
                split(s, at, b)
                if j == 0:
                    norm_high(norm_c2)
            gate_up(gc_b, KD, T, func=ACT.Sigmoid)
            for b, j, s, at in stage(act, ga_b, KD // 2):
                split(s, at, b)
                act.wait_ge(pe_done, b + 1)
                for half in range(2):
                    o = GA[:, ds(j * 2 + half, 1), :].rearrange("p a t -> p (a t)")
                    last = act.activation(o, (G, U)[half][s][:, :], ACT.Sigmoid)
                last.then_inc(ga_done, 1)
            for b in range(q_b, k_b + 1):
                split(b % 2, loaded(b, 1), b)
                act.wait_ge(pe_done, b + 1)
                for wave in hn_waves(b):
                    for i in wave:
                        tok = HN[i][3]
                        if i >= 2:
                            act.wait_ge(hn_z, i - 1)
                        act.activation(SA[:, i % 2, 0:tok], hn_bank(i), ACT.Square).then_inc(hn_sq, 1)
                    for i in wave:
                        tok = HN[i][3]
                        act.wait_ge(hn_mm, i + 1)
                        act.activation(SA[:, i % 2, 0:tok], B[4 + i % 2][:, 0:tok], ACT.Sqrt, bias=eps[:, :],
                                       scale=1.0 / P).then_inc(hn_rms, 1)
            split(v2_b % 2, loaded(v2_b, 1), v2_b)

            def exp2(u):
                act.wait_ge(at2_m, u + 1)
                if u >= 4:
                    act.wait_ge(at2_t, 2 * (u - 3))
                act.activation(p_slot2(u), PS[:, (u % 2) * 1024:(u % 2) * 1024 + TK], ACT.Exp,
                               bias=stat(NM, u), scale=float(P) ** -0.5, accum_out=stat(DEN, u)).then_inc(at2_e, 1)

            def turned2(u):
                n = u // 4
                for x in range(2):
                    act.wait_ge(at2_t, 2 * u + x + 1)
                    if u % 4 == 0 and x == 0 and n:
                        act.wait_ge(at2_v, n)
                    act.activation(PT2[:, 3 * x:3 * x + 3, u % 4, :],
                                   B[4 + (2 * u + x) % 3][:, 0:3 * P].rearrange("p (t q) -> p t q", q=P),
                                   ACT.Copy).then_inc(at2_c, 1)

            def heads2(n):
                act.wait_ge(at2_v, n + 1)
                g, q = n // NT, n % NT
                act.activation(NH[:, g * 4:g * 4 + 4, q * P:(q + 1) * P],
                               B[7][:, :].rearrange("p (h q) -> p h q", h=4), ACT.Copy).then_inc(at2_h, 1)

            for u in range(1 - AHEAD, len(UNITS2)):
                if u + AHEAD - 1 < len(UNITS2):
                    exp2(u + AHEAD - 1)
                if u >= 0:
                    if u % 4 == 0 and u:
                        heads2(u // 4 - 1)
                    turned2(u)
            heads2(len(UNITS2) // 4 - 1)
            only_split(ba_b, KD // 2)
            only_split(wo2_b, KD // 2)
            norm(norm_x3)
            ffn(ffn4, T, True)
            norm(norm_out)

        @block.vector
        def _(dve):
            own = Count(dve_s)

            def split(s, b):
                dve.wait_ge(w_hi, b + 2)
                dve.tensor_tensor(WL[1 - s][:, :], RAW[1 - s][:, :], WH[1 - s][:, :].bitcast(F32),
                                  ALU.subtract).then_inc(w_lo, 1)

            def norm(m):
                dve.wait_ge(norm_rms, m.no + 1)
                own.settle(dve, dve.reciprocal(roots(m), roots(m)))

                def low(k):
                    dve.wait_ge(norm_hi, m.low + k + 1)
                    h, l = m.dst(k)
                    if m.shift:
                        ins = dve.scalar_tensor_tensor(out=l, in0=VA[:, k % 2, 0:m.tok], scalar=m.shift(k),
                                                       in1=h.bitcast(F32), op0=ALU.add, op1=ALU.subtract)
                    else:
                        ins = dve.tensor_tensor(l, VA[:, k % 2, 0:m.tok], h.bitcast(F32), ALU.subtract)
                    ins.then_inc(norm_lo, 1)

                for k in range(m.n):
                    if m.dst and k >= 2:
                        dve.wait_ge(norm_lo, m.low + k - 1)
                    o = VA[:, k % 2, 0:m.tok] if m.dst else m.src(k)
                    dve.scalar_tensor_tensor(out=o, in0=m.src(k), scalar=m.gain(k), in1=roots(m),
                                             op0=ALU.mult, op1=ALU.mult).then_inc(norm_x, 1)
                    if m.dst and k:
                        low(k - 1)
                if m.dst:
                    low(m.n - 1)

            def mods(b0, j, s, m0):
                if m0 is None:
                    return
                t = (s + b0) % 2
                dve.wait_ge(mod_loaded[t], j * 8 + (8 * (m0 - t) + 16))
                for k in range(KD):
                    if k:
                        dve.wait_ge(mod_s, j * KD + (KD * m0 + k))
                    for v in range(vectors(m0)):
                        o = MACC[:, t, v, :]
                        if k:
                            last = dve.scalar_tensor_tensor(out=o, in0=MW[t][:, k, :], scalar=CV2[:, k, v:v + 1],
                                                            in1=o, op0=ALU.mult, op1=ALU.add)
                        else:
                            last = dve.tensor_scalar(o, MW[t][:, k, :], CV2[:, k, v:v + 1], None, ALU.mult)
                    last.then_inc(mod_s, 1)

            def mods_out(b0, j, s, m0):
                if m0 is None:
                    return
                dve.wait_ge(mod_done, j + (m0 + 1))
                nv = vectors(m0)
                dve.tensor_copy(MOD[:, ds(j + m0, 1), 0:nv].rearrange("p a b -> p (a b)"),
                                B[4 + (s + b0) % 2][:, 0:nv]).then_inc(mod_out, 1)

            def gate_up(b0, n, tok, g0, h0, m0=None):
                for b, j, s, at in stage(dve, b0, n):
                    mods(b0, j, s, m0)
                    split(s, b)
                    dve.wait_ge(gate_done, j + (g0 + 1))
                    wait(dve, h_split, after(j + h0, -1))
                    if tok > T:
                        dve.tensor_tensor(VA[:, s, T:tok], SA[:, s, T:tok], CU[s][:, 0:tok - T], ALU.mult)
                    dve.tensor_tensor(VA[:, s, 0:T], SA[:, s, 0:T], U[s][:, :], ALU.mult).then_inc(psum_free, 1)
                    mods_out(b0, j, s, m0)

            def down(b0, tok, by, by_ctx, straight=False, m0=None):
                for b, j, s, at in stage(dve, b0, KD // 2, straight):
                    mods(b0, j, s, m0)
                    if at is not None:
                        split(s, b)
                    dve.wait_ge(pe_done, b + 1)
                    dve.wait_ge(psum_free, b)
                    for half, bank in enumerate((G, U)):
                        if tok > T:
                            o = CX[:, ds(j * 2 + half, 1), :].rearrange("p a t -> p (a t)")
                            dve.scalar_tensor_tensor(out=o, in0=(CG, CU)[half][s][:, 0:tok - T],
                                                     scalar=by_ctx(j * 2 + half), in1=o, op0=ALU.mult, op1=ALU.add)
                        o = X[:, ds(j * 2 + half, 1), :].rearrange("p a t -> p (a t)")
                        last = dve.scalar_tensor_tensor(out=o, in0=bank[s][:, :], scalar=by(j * 2 + half), in1=o,
                                                        op0=ALU.mult, op1=ALU.add)
                    last.then_inc(psum_free, 1)
                    mods_out(b0, j, s, m0)

            def ffn(stages, tok, name, by, by_ctx=None, last=False):
                g0, h0, m0 = G0[name], H0[name], M0.get(name)
                for c, (kn, (bg, bd)) in enumerate(zip(CHUNKS, stages)):
                    gate_up(bg, kn, tok, g0, h0, m0)
                    m1 = None if m0 is None else m0 + kn
                    down(bd, tok, by, by_ctx, last and c == 2, m1)
                    m0 = None if m0 is None else m1 + KD // 2
                    g0, h0 = g0 + kn, h0 + kn

            def transposed(no, dst_of):
                for t in range(32):
                    dve.wait_ge(tp_done, no * 32 + t + 1)
                    dve.tensor_copy(dst_of(t), B[t % 4][:, 0:P]).then_inc(tp_out, 1)

            dve.memset(ones[:, :], 1.0).then_inc(c2_s, 1)
            dve.wait_ge(c2_s, 1)
            dve.memset(eps[:, :], EPS).then_inc(c2_s, 1)
            dve.wait_ge(v_loaded, 16)
            transposed(0, lambda t: X[:, t % KD, (t // KD) * P:(t // KD + 1) * P])
            dve.wait_ge(w_hi, 1)
            dve.tensor_tensor(WL[0][:, :], RAW[0][:, :], WH[0][:, :].bitcast(F32), ALU.subtract).then_inc(w_lo, 1)
            norm(norm1)
            dve.wait_ge(act_s, 1)
            ffn(ffn1, T, "ffn1", lambda t: 0.5)
            norm(norm_mix)
            dve.wait_ge(a_loaded, 64)
            own.settle(dve, dve.memset(VAP[:, :, :, :], 0.0))
            for n in range(10):
                b = w_in_b + n
                s = b % 2
                split(s, b)
                dve.wait_ge(pe_done, b + 1)
                for i, half in enumerate(COPIED[n], COPY0[n]):
                    dve.wait_ge(rope_y, i + 1)
                for kind, half, _ in ITEMS[n]:
                    y = (G, U)[half][s]
                    if kind == "rope":
                        own.settle(dve, dve.tensor_tensor(VA[:, half, 0:T], y[:, :], TA[:, 0, :], ALU.mult))
                    if kind == "kr":
                        own.settle(dve, dve.tensor_tensor(KPE[64:96, :], y[64:96, :], TB[64:96, 0, :], ALU.mult))
                for half, t in enumerate(W_IN_TILES[2 * n:2 * n + 2]):
                    if t[0] == "lat":
                        own.settle(dve, dve.tensor_copy(CQ[:, t[1], :], (G, U)[half][s][:, :]))
                        dve.sem_inc(lat_out, 1)
                dve.sem_inc(psum_free, 1)
                for i, (kind, half, dst) in enumerate(ITEMS[n], ITEM0[n]):
                    dve.wait_ge(rope_mm, i + 1)
                    o = B[4 + i % 2]
                    if kind in ("wi", "va"):
                        turned = o[:, :].rearrange("p (t c) -> p t c", c=P)
                    if kind == "wi":
                        ins = dve.tensor_scalar(WI[:, :, :], turned[:, :, 96:96 + IDX_HEADS],
                                                float(IDX_HEADS * 64) ** -0.5, None, ALU.mult)
                    elif kind == "va":
                        dve.tensor_copy(VAP[:, :, 0, 0:64], turned[:, :, 64:128])
                        ins = dve.tensor_copy(VAP[:, :, 1, 64:128], turned[:, :, 64:128])
                    else:
                        r, tab = (slice(64, 96), TB) if kind == "kr" else (slice(0, P), TA)
                        if kind == "twice":
                            own.settle(dve, dve.tensor_tensor(VA[:, half, 0:T], B[6 + i % 2][:, :], TA[:, 0, :], ALU.mult))
                        own.settle(dve, dve.tensor_tensor(RB[r, :], o[r, :], tab[r, 1, :], ALU.mult))
                        a, d = (KPE[r, :], KPE[r, :]) if kind == "kr" else (VA[r, half, 0:T], dst)
                        ins = dve.tensor_tensor(d, a, RB[r, :], ALU.add)
                    ins.then_inc(rope_out, 1)
                    dve.wait_ge(rope_out, i + 1)
            norm(norm_q)
            norm(norm_kv)

            n = 0
            for q in range(1, NT):
                keys = (q + 1) * P
                acc = BIAS[:, q - 1, 0:keys]
                for h in range(IDX_HEADS):
                    dve.wait_ge(ix_relu, n + 1)
                    if n:
                        dve.wait_ge(ix_acc, n)
                    dve.scalar_tensor_tensor(out=acc, in0=SA[:, n % 2, 0:keys], scalar=WI[:, q, h:h + 1],
                                             in1=acc if h else CM[:, (NT - 1 - q) * P:T],
                                             op0=ALU.mult, op1=ALU.add).then_inc(ix_acc, 1)
                    n += 1

            def select():
                for q in range(1, NT):
                    acc = BIAS[:, q - 1, 0:(q + 1) * P]
                    for r in range(TOPK // 8):
                        own.inc(dve.max(M8[:, :], acc))
                        n = own.n
                        yield
                        dve.wait_ge(dve_s, n)
                        own.inc(dve.match_replace(acc, M8[:, :], acc, 3 * NEG * 1e7))
                        n = own.n
                        yield
                        dve.wait_ge(dve_s, n)
                    own.settle(dve, dve.tensor_scalar(acc, acc, 2 * NEG * 1e7, NEG, ALU.is_gt, ALU.mult))

            split(v_b % 2, v_b)
            dve.wait_ge(ix_acc, n)
            dve.wait_ge(v_zero, 1)
            for t in range(NT):
                dve.wait_ge(v_mm, t + 1)
                v = B[2 + t % 2][:, :].rearrange("p (h b c) -> p h b c", h=4, b=2)
                o = VB[:, t, :, :].rearrange("p (h b) c -> p h b c", b=2)
                dve.tensor_copy(o[:, :, 0, 0:64], v[:, :, 0, :])
                dve.tensor_copy(o[:, :, 1, 64:128], v[:, :, 1, :]).then_inc(v_out, 1)
            dve.wait_ge(v_out, NT)
            dve.sem_inc(psum_free, 1)
            for i in range(4):
                own.settle(dve, dve.tensor_copy(KB[64:96, i, :], KPE[64:96, :]))

            def project(n):
                b = pj_b + n
                split(b % 2, b)
                for i in range(4):
                    dve.wait_ge(pj_mm, 4 * n + i + 1)
                    dve.tensor_copy(KB[0:64, i, :], B[7][0:64, :]).then_inc(pj_k, 1)
                    dve.wait_ge(pj_y, 4 * n + i + 1)
                    own.settle(dve, dve.tensor_tensor(RB[0:96, :], pj_bank(i), TB[0:96, 0, :], ALU.mult))
                    dve.wait_ge(pj_sw, 4 * n + i + 1)
                    own.settle(dve, dve.tensor_tensor(QB[0:96, i, :], B[4][0:96, :], TB[0:96, 1, :], ALU.mult))
                    dve.tensor_tensor(QB[0:96, i, :], QB[0:96, i, :], RB[0:96, :], ALU.add).then_inc(pj_out, 1)
                    dve.wait_ge(pj_out, 4 * n + i + 1)
                dve.sem_inc(psum_free, 1)

            def masked(u):
                kind, h, q = UNITS[u]
                keys = (q + 1) * P
                dve.wait_ge(at_s, u + 1)
                if u >= 4:
                    dve.wait_ge(at_t, u - 3)
                bias = CM[:, (NT - 1 - q) * P:T] if kind == "b" or q == 0 else BIAS[:, q - 1, 0:keys]
                scale = float(96 if kind == "b" else 64) ** -0.5
                own.inc(dve.tensor_tensor_reduce(out=p_slot(u)[:, 0:keys], in0=B[u % 2][:, 0:keys], in1=bias,
                                                 scale=scale, scalar=3 * NEG * 1e7, op0=ALU.add, op1=ALU.max,
                                                 accum_out=stat(NM, u)))
                return own.n

            def negated(u, n):
                dve.wait_ge(dve_s, n)
                dve.tensor_scalar(stat(NM, u), stat(NM, u), -1.0, None, ALU.mult).then_inc(at_m, 1)

            def inverse(u):
                dve.wait_ge(at_e, u + 1)
                dve.reciprocal(stat(DEN, u), stat(DEN, u)).then_inc(at_d, 1)

            def heads(g):
                dve.wait_ge(at_h, g + 1)
                i = B[4][:, :] if g < 4 else B[4][:, :].rearrange("p (h q) -> p h q", h=4)
                dve.tensor_tensor(heads_out(g, NL), i, heads_out(g, NH).bitcast(F32), ALU.subtract).then_inc(at_o, 1)

            selection = select()
            ROUNDS = TOPK // 8
            assert all(32 + HA * q - AHEAD > ROUNDS * q for q in range(1, NT))
            for u in range(-AHEAD, len(UNITS)):
                if 0 <= u + 1 < len(UNITS):
                    inverse(u + 1)
                if u + AHEAD in (0, 16):
                    project((u + AHEAD) // 16)
                if u + AHEAD == len(UNITS) - HA:
                    for _ in selection:
                        pass
                if u >= 0:
                    next(selection, None)
                n = masked(u + AHEAD) if u + AHEAD < len(UNITS) else None
                if u >= 0:
                    next(selection, None)
                if n is not None:
                    negated(u + AHEAD, n)
                if u >= 0:
                    if u % PER_GROUP == 1 and u > 1:
                        heads(u // PER_GROUP - 1)
            heads(NG - 1)
            down(wo_b, T, lambda t: 1.0, None, m0=M0["wo"])
            norm(norm2)
            ffn(ffn2, T, "ffn2", lambda t: 0.5)
            dve.wait_ge(mod_out, NMOD * KD)
            c = VEC["b_mod"][0]
            for v, n in enumerate((NMOD * KD, NCTX)):
                own.settle(dve, dve.tensor_tensor(MOD[:, 0:n, v], MOD[:, 0:n, v], vecs[:, c:c + n], ALU.add))
            for n, (name, i, v) in enumerate(MODULATED):
                own.inc(dve.scalar_tensor_tensor(out=GS[:, n, :], in0=MOD[:, i * KD:(i + 1) * KD, v], scalar=1.0,
                                                 in1=vecs[:, VEC[name][0]:VEC[name][0] + KD], op0=ALU.add,
                                                 op1=ALU.mult))
            for n, (i, v) in enumerate(HALVED):
                own.settle(dve, dve.tensor_scalar(HG[:, n, :], MOD[:, i * KD:(i + 1) * KD, v], 0.5, None, ALU.mult))
            norm(norm_final)

            norm(norm_c1)
            dve.wait_ge(norm_x, norm_final.base + KD)
            norm(norm_x1)
            ffn(ffn3, T + TC, "ffn3", lambda t: HG[:, 0, ds(t, 1)], lambda t: HG[:, 1, ds(t, 1)])
            norm(norm_x2)
            dve.wait_ge(norm_lo, norm_x2.low + KD)
            dve.memset(VA[:, :, 0:T + 2], 0.0).then_inc(conv_s, 1)
            for b, j, s, at in stage(dve, conv_b, KD):
                split(s, b)
                dve.wait_ge(gate_done, j + (G0["conv"] + 1))
                dve.wait_ge(conv_s, j * 3 + 1)
                dve.tensor_tensor(VA[:, s, 1:T + 1], SA[:, s, 0:T], U[s][:, :], ALU.mult).then_inc(psum_free, 1)
                dve.wait_ge(psum_free, b + 1)
                o = M[:, ds(j, 1), :].rearrange("p a t -> p (a t)")
                for tap in range(3):
                    w = vecs[:, ds(j + (VEC["conv"][0] + tap * KD), 1)]
                    src = VA[:, s, tap:tap + T]
                    if tap == 0:
                        dve.tensor_scalar(o, src, w, None, ALU.mult).then_inc(conv_s, 1)
                    else:
                        dve.wait_ge(conv_s, j * 3 + (tap + 1))
                        dve.scalar_tensor_tensor(out=o, in0=src, scalar=w, in1=o, op0=ALU.mult, op1=ALU.add)\
                            .then_inc(conv_s, 1)
            dve.wait_ge(conv_s, 3 * KD + 1)
            for b, j, s, at in stage(dve, bg_b, KD // 2, True):
                split(s, b)
                if j == 0:
                    norm(norm_c2)
                    dve.wait_ge(norm_lo, norm_c2.low + KD)
                dve.wait_ge(pe_done, b + 1)
                if j:
                    dve.wait_ge(y_split, 2 * j)
                for half in range(2):
                    last = dve.tensor_tensor(VA[:, half, 0:T], (G, U)[half][s][:, :], M[:, 2 * j + half, :], ALU.mult)
                last.then_inc(psum_free, 1)
            dve.wait_ge(psum_free, gc_b)
            for b, j, s, at in stage(dve, gc_b, KD):
                split(s, b)
                dve.wait_ge(gate_done, j + (G0["gc"] + 1))
                dve.wait_ge(pe_done, b + 1)
                dve.tensor_tensor(M[:, ds(j, 1), :].rearrange("p a t -> p (a t)"), SA[:, s, 0:T], U[s][:, :],
                                  ALU.mult).then_inc(psum_free, 1)
            for b, j, s, at in stage(dve, ga_b, KD // 2):
                split(s, b)
                dve.wait_ge(ga_done, j + 1)
                dve.sem_inc(psum_free, 1)
            dve.wait_ge(b_loaded, 32)
            for b in range(q_b, k_b + 1):
                split(b % 2, b)
                for wave in hn_waves(b):
                    for i in wave:
                        tok = HN[i][3]
                        dve.wait_ge(hn_rms, i + 1)
                        own.settle(dve, dve.reciprocal(SA[:, i % 2, 0:tok], SA[:, i % 2, 0:tok]))
                        if i >= 2:
                            dve.wait_ge(hn_out, i - 1)
                        o = VA[:, i % 2, 0:tok] if tok == T else HN[i][5]
                        dve.scalar_tensor_tensor(out=o, in0=hn_bank(i), scalar=vec(HN[i][4]), in1=SA[:, i % 2, 0:tok],
                                                 op0=ALU.mult, op1=ALU.mult).then_inc(hn_z, 1)
                    dve.wait_ge(hn_z, i + 1)
                    if wave[-1] == hn_of(b)[-1]:
                        dve.sem_inc(psum_free, 1)
                    for i in wave:
                        if HN[i][3] == T:
                            own.settle(dve, dve.tensor_tensor(RB[:, :], VA[:, i % 2, 0:T], TX[:, 0, :], ALU.mult))
                            dve.wait_ge(hn_sw, i + 1)
                            own.settle(dve, dve.tensor_tensor(HN[i][5], B[6 + i % 2], TX[:, 1, :], ALU.mult))
                            own.settle(dve, dve.tensor_tensor(HN[i][5], HN[i][5], RB[:, :], ALU.add))
                        dve.sem_inc(hn_out, 1)
            split(v2_b % 2, v2_b)
            for t in range(TK // P):
                dve.wait_ge(v2_mm, t + 1)
                dve.tensor_copy(V2[:, t, :], B[t % 4][:, 0:2 * P]).then_inc(v2_out, 1)
            dve.wait_ge(v2_out, TK // P)
            dve.sem_inc(psum_free, 1)

            def maximum2(u):
                dve.wait_ge(at2_s, u + 1)
                if u >= 4:
                    dve.wait_ge(at2_e, u - 3)
                nm = stat(NM, u)
                own.settle(dve, dve.tensor_reduce(nm, PS[:, (u % 2) * 1024:(u % 2) * 1024 + TK], AX.X, ALU.max,
                                                  negate=True))
                dve.tensor_scalar(nm, nm, float(P) ** -0.5, None, ALU.mult).then_inc(at2_m, 1)

            def normalised2(u):
                d = stat(DEN, u)
                dve.wait_ge(at2_e, u + 1)
                own.settle(dve, dve.reciprocal(d, d))
                p = p_slot2(u)
                dve.tensor_scalar(p, p, d, None, ALU.mult).then_inc(at2_r, 1)

            def heads2(n):
                dve.wait_ge(at2_h, n + 1)
                g, q = n // NT, n % NT
                h, l = (z[:, g * 4:g * 4 + 4, q * P:(q + 1) * P] for z in (NH, NL))
                dve.tensor_tensor(l, B[7][:, :].rearrange("p (h q) -> p h q", h=4), h.bitcast(F32), ALU.subtract)\
                    .then_inc(at2_o, 1)

            for u in range(-AHEAD, len(UNITS2)):
                if u >= 0:
                    normalised2(u)
                if u + AHEAD < len(UNITS2):
                    maximum2(u + AHEAD)
                if u % 4 == 1 and u > 1:
                    heads2(u // 4 - 1)
            heads2(len(UNITS2) // 4 - 1)
            for b, j, s, at in stage(dve, ba_b, KD // 2, True):
                split(s, b)
                dve.wait_ge(pe_done, b + 1)
                if j:
                    dve.wait_ge(y_split, KD + 2 * j)
                for half in range(2):
                    own.inc(dve.tensor_tensor(VA[:, half, 0:T], (G, U)[half][s][:, :], GA[:, 2 * j + half, :], ALU.mult))
                for half in range(2):
                    dve.wait_ge(dve_s, own.n)
                    last = dve.tensor_tensor(VA[:, half, 0:T], VA[:, half, 0:T], M[:, 2 * j + half, :], ALU.add)
                last.then_inc(psum_free, 1)
            down(wo2_b, T, lambda t: mod(5, t, 0), None)
            norm(norm_x3)
            ffn(ffn4, T, "ffn4", lambda t: HG[:, 2, ds(t, 1)], None, True)
            norm(norm_out)
            transposed(1, lambda t: XIN[:, t // KD, (t % KD) * P:(t % KD + 1) * P])

        @block.gpsimd
        def _(pool):
            def hidden(b0, n, tok, g0):
                for b, j, s, _ in stage(pool, b0, n):
                    pool.wait_ge(psum_free, b + 1)
                    h = HH[:, ds(j, 1), 0:tok].rearrange("p a t -> p (a t)")
                    l = HL[:, ds(j, 1), 0:tok].rearrange("p a t -> p (a t)")
                    pool.tensor_copy(h, VA[:, s, 0:tok]).then_inc(pool_s, 1)
                    pool.wait_ge(pool_s, j + (g0 + 1))
                    pool.tensor_tensor(l, VA[:, s, 0:tok], h.bitcast(F32), ALU.subtract).then_inc(h_split, 1)

            def ffn(stages, tok, g0):
                for kn, (bg, bd) in zip(CHUNKS, stages):
                    hidden(bg, kn, tok, g0)
                    g0 += kn

            def branch(b0, h_to, l_to, y0):
                for b, j, s, _ in stage(pool, b0, KD // 2, True):
                    pool.wait_ge(psum_free, b + 1)
                    for half in range(2):
                        t = 2 * j + half
                        pool.tensor_copy(h_to[:, t, :], VA[:, half, 0:T]).then_inc(y_part, 1)
                        pool.wait_ge(y_part, y0 + t + 1)
                        pool.tensor_tensor(l_to[:, t, :], VA[:, half, 0:T], h_to[:, t, :].bitcast(F32), ALU.subtract)\
                            .then_inc(y_split, 1)

            def norm(m):
                for k in range(1, m.n - 2):
                    pool.wait_ge(norm_sq, m.base + k + 1)
                    if k > 1:
                        pool.wait_ge(norm_acc, m.acc + k - 1)
                    pool.tensor_tensor(squares(m, 0), squares(m, 0), squares(m, k), ALU.add).then_inc(norm_acc, 1)

            ffn(ffn1, T, 0)
            norm(norm_mix)
            pool.wait_ge(ix_acc, 3 * IDX_HEADS)
            pool.memset(VB[:, :, :, :], 0.0).then_inc(v_zero, 1)
            norm(norm2)
            ffn(ffn2, T, H0["ffn2"])
            norm(norm_final)
            ffn(ffn3, T + TC, H0["ffn3"])
            norm(norm_x2)
            branch(bg_b, YH, YL, 0)
            branch(ba_b, MH, ML, KD)
            norm(norm_x3)
            ffn(ffn4, T, H0["ffn4"])
            norm(norm_out)


def _vectors(inputs):
    import numpy as np
    named = {"g_ffn1": "g_ffn1", "g_mix": "g_mix", "g_ffn2": "g_ffn2", "g_final": "g_final", "g_q_lat": "g_q_lat",
             "g_kv_lat": "g_kv_lat", "norm1": "norm1_g_2", "norm2": "norm2_g_2", "norm3": "norm3_g_2",
             "final": "final_g_2", "q_norm": "q_norm_g_2", "k_norm": "k_norm_g_2", "b_mod": "b_mod_2",
             "conv": "conv_w_2", "c": "c_2", "c_ctx": "c_ctx_2"}
    return np.ascontiguousarray(np.concatenate(
        [np.asarray(inputs[named[n]]).reshape(-1, P).T for n in VEC], axis=1))


def _constants():
    import numpy as np
    f32 = np.float32

    def rope(dim):
        inv = f32(10000.0) ** (-np.arange(0, dim, 2, dtype=f32) / f32(dim))
        ang = (np.arange(T, dtype=f32)[:, None] * inv[None, :]).T
        return np.cos(ang), np.sin(ang)

    c, s = rope(64)
    rope64 = np.stack([np.tile(c, (4, 1)), np.concatenate([-s, s, -s, s])], 1)
    c, s = rope(32)
    rope96 = np.zeros((P, 2, T), f32)
    rope96[:64, 0] = 1.0
    rope96[64:96, 0] = np.concatenate([c, c])
    rope96[64:96, 1] = np.concatenate([-s, s])
    perms = np.zeros((P, 4, P), f32)
    for r in range(P):
        perms[r ^ 32, 0, r] = 1
        perms[r % 64, 1, r] = 1
        perms[(r % 64) ^ 32, 2, r] = 1
    for r in range(64, 96):
        perms[r ^ 16, 3, r] = 1
    inv = f32(10000.0) ** (-np.arange(32, dtype=f32) / f32(32))
    t = np.arange(T)
    ang = [(z.astype(f32)[:, None] * inv).T for z in (t // 64, t % 64)]
    rope128 = np.stack([np.concatenate([np.cos(a) for a in ang for _ in range(2)]),
                        np.concatenate([f(np.sin(a)) for a in ang for f in (np.negative, np.positive)])], 1)
    q, k = np.arange(P)[:, None], np.arange(P)[None, :]
    causal = np.zeros((P, T), f32)
    causal[:, T - P:] = np.where(k <= q, 0.0, NEG)
    return {"ident": np.eye(P, dtype=f32), "rope64": rope64.astype(f32), "rope96": rope96, "perms": perms,
            "causal": causal, "rope128": rope128.astype(f32)}


_WEIGHTS = ["x", "w1_gate", "w1_up", "w1_down", "w_in", "w_uq", "w_ukv", "w_out", "w2_gate", "w2_up", "w2_down",
            "ctx_2", "w_mod_2", "ffn1_w_in_2", "ffn1_w_out_2", "w_in_2", "w_branch_conv_2", "w_branch_attn_2", "w_out_2",
            "ffn2_w_in_2", "ffn2_w_out_2"]
_OUT = (1, 512, 1024)


def kernel(**inputs):
    import numpy as np
    import concourse.bacc as bacc
    from concourse.bass_utils import run_bass_kernel_spmd

    nc = bacc.Bacc("TRN2", target_bir_lowering=False, num_devices=1)
    given = {n: np.ascontiguousarray(inputs[n]) for n in _WEIGHTS}
    given["vecs"] = _vectors(inputs)
    given.update(_constants())
    arrays, aps = {}, {}
    for name, a in given.items():
        arrays[f"in_{name}"] = a
        aps[name] = nc.dram_tensor(f"in_{name}", a.shape, mybir.dt.from_np(a.dtype), kind="ExternalInput").ap()
    out = nc.dram_tensor("out_0", _OUT, F32, kind="ExternalOutput").ap()
    build(nc, aps, out)
    r = run_bass_kernel_spmd(nc, [arrays], core_ids=[0])
    return r.results[0]["out_0"]
```
